# Optimizing a Trainium2 kernel written in Bass

```python
import math
import jax, jax.numpy as jnp
from jax import lax
import numpy as np

D_MODEL = 1024
BATCH = 1
SEQ = 128
DEPTH = 2
DEC_BATCH = 1
DEC_SEQ = 512
PAST_LEN = 128

GRID_W = 64
HEAD_DIM = 64
MIX_WIDTH = D_MODEL
GROUP_WIDTH = MIX_WIDTH // 4
N_HEADS_A = GROUP_WIDTH // HEAD_DIM
KV_HEADS_A = 2
Q_PER_KV = N_HEADS_A // KV_HEADS_A
N_HEADS_C = GROUP_WIDTH // HEAD_DIM
N_FOURIER_GROUPS = GROUP_WIDTH // HEAD_DIM
FOURIER_GROUP_DIM = HEAD_DIM
SHORT_CONV = 3
DELTA_CHUNK = 64
Q_BLOCK = 128
ROPE_THETA = 10000.0
D_FF = 2816
N_MOD = 9
EPS = 1e-6
SPLIT_SIZES = (N_HEADS_A * HEAD_DIM, KV_HEADS_A * HEAD_DIM, KV_HEADS_A * HEAD_DIM,
               GROUP_WIDTH, GROUP_WIDTH, GROUP_WIDTH,
               GROUP_WIDTH, GROUP_WIDTH, GROUP_WIDTH, GROUP_WIDTH,
               N_HEADS_C, N_HEADS_C, N_HEADS_C, N_HEADS_C,
               GROUP_WIDTH)
PROJ_WIDTH = sum(SPLIT_SIZES)

kernel_name = 'hybrid_diffusion_parallel_groups_step'

def split_cols(t):
    offs = [int(o) for o in np.cumsum(SPLIT_SIZES)[:-1]]
    return jnp.split(t, offs, axis=-1)

def rms_norm(x, g):
    x32 = x.astype(jnp.float32)
    y = x32 * lax.rsqrt(jnp.mean(x32 * x32, axis=-1, keepdims=True) + EPS)
    return (y * g.astype(jnp.float32)).astype(x.dtype)

def l2_norm(x):
    return x * lax.rsqrt(jnp.sum(x * x, axis=-1, keepdims=True) + EPS)

def rope_2d(x):
    L = x.shape[1]
    rows = L // GRID_W
    r, cl = jnp.meshgrid(jnp.arange(rows), jnp.arange(GRID_W), indexing='ij')
    pos_r = r.reshape(-1).astype(jnp.float32)
    pos_c = cl.reshape(-1).astype(jnp.float32)
    quarter = HEAD_DIM // 4
    half = HEAD_DIM // 2
    inv_freq = ROPE_THETA ** (-jnp.arange(quarter, dtype=jnp.float32) / quarter)

    def rot(xh, pos):
        ang = pos[:, None] * inv_freq[None, :]
        cos = jnp.cos(ang)[None, :, None, :].astype(x.dtype)
        sin = jnp.sin(ang)[None, :, None, :].astype(x.dtype)
        x1, x2 = xh[..., :quarter], xh[..., quarter:]
        return jnp.concatenate([x1 * cos - x2 * sin, x2 * cos + x1 * sin], axis=-1)

    return jnp.concatenate([rot(x[..., :half], pos_r), rot(x[..., half:], pos_c)], axis=-1)

def block_attention(q, k, v):
    Bn, Lq = q.shape[0], q.shape[1]
    nb = Lq // Q_BLOCK
    qb = jnp.moveaxis(q.reshape(Bn, nb, Q_BLOCK, KV_HEADS_A, Q_PER_KV, HEAD_DIM), 1, 0)
    scale = HEAD_DIM ** -0.5

    def one_block(qi):
        s = jnp.einsum('bqhgd,bkhd->bhgqk', qi, k).astype(jnp.float32) * scale
        p = jax.nn.softmax(s, axis=-1).astype(v.dtype)
        return jnp.einsum('bhgqk,bkhd->bqhgd', p, v)

    o = lax.map(one_block, qb)
    return jnp.moveaxis(o, 0, 1).reshape(Bn, Lq, N_HEADS_A * HEAD_DIM)

def depthwise_conv(u, w):
    K = w.shape[0]
    pad = K // 2
    L = u.shape[1]
    up = jnp.pad(u, ((0, 0), (pad, pad), (0, 0)))
    y = up[:, 0:L] * w[0]
    for j in range(1, K):
        y = y + up[:, j:j + L] * w[j]
    return y

def chunk_gated_delta(q, k, v, g, beta, s0):
    Bn, H, L, dk = q.shape
    dv = v.shape[-1]
    C = DELTA_CHUNK
    n = L // C
    q = q.reshape(Bn, H, n, C, dk)
    k = k.reshape(Bn, H, n, C, dk)
    v = v.reshape(Bn, H, n, C, dv)
    g = g.reshape(Bn, H, n, C)
    beta = beta.reshape(Bn, H, n, C)
    gc = jnp.cumsum(g, axis=-1)
    idx = jnp.arange(C)
    incl = idx[:, None] >= idx[None, :]
    strict = idx[:, None] > idx[None, :]
    decay = jnp.exp(jnp.where(incl, gc[..., :, None] - gc[..., None, :], -jnp.inf))
    kb = k * beta[..., None]
    vb = v * beta[..., None]
    lmat = jnp.where(strict, jnp.einsum('bhncd,bhnjd->bhncj', kb, k) * decay, 0.0)
    eye = jnp.eye(C, dtype=jnp.float32)
    t_inv = lax.linalg.triangular_solve(eye + lmat, jnp.broadcast_to(eye, lmat.shape),
                                        left_side=True, lower=True, unit_diagonal=True)
    u = t_inv @ vb
    w = t_inv @ (kb * jnp.exp(gc)[..., None])
    aqk = jnp.einsum('bhncd,bhnjd->bhncj', q, k) * decay
    qg = q * jnp.exp(gc)[..., None]
    kdec = k * jnp.exp(gc[..., -1:] - gc)[..., None]
    glast = jnp.exp(gc[..., -1])

    def step(S, xs):
        u_c, w_c, qg_c, aqk_c, kdec_c, gl = xs
        v_new = u_c - w_c @ S
        o_c = qg_c @ S + aqk_c @ v_new
        S = S * gl[..., None, None] + jnp.swapaxes(kdec_c, -1, -2) @ v_new
        return S, o_c

    xs = tuple(jnp.moveaxis(a, 2, 0) for a in (u, w, qg, aqk, kdec, glast))
    S, o = lax.scan(step, s0, xs)
    o = jnp.moveaxis(o, 0, 2).reshape(Bn, H, L, dv)
    return o, S

def gated_deltanet(qc, kc, vc, zc, beta_f, beta_b, a_f, a_b, conv_w, a_log, dt_bias, norm_g, s0):
    f32 = jnp.float32
    Bn, L, _ = qc.shape
    qkv = jax.nn.silu(depthwise_conv(jnp.concatenate([qc, kc, vc], axis=-1), conv_w).astype(f32))
    q, k, v = jnp.split(qkv, 3, axis=-1)

    def heads(t):
        return jnp.swapaxes(t.reshape(Bn, L, N_HEADS_C, HEAD_DIM), 1, 2)

    q = l2_norm(heads(q)) * HEAD_DIM ** -0.5
    k = l2_norm(heads(k))
    v = heads(v)
    decay_rate = jnp.exp(a_log.astype(f32))
    dtb = dt_bias.astype(f32)

    def gates(b_raw, a_raw, d):
        beta = jax.nn.sigmoid(b_raw.astype(f32))
        g = -decay_rate[d] * jax.nn.softplus(a_raw.astype(f32) + dtb[d])
        return jnp.swapaxes(beta, 1, 2), jnp.swapaxes(g, 1, 2)

    bf, gf = gates(beta_f, a_f, 0)
    bb, gb = gates(beta_b, a_b, 1)
    s0 = s0.astype(f32)
    o_f, s_f = chunk_gated_delta(q, k, v, gf, bf, s0[:, 0])

    def rev(t):
        return jnp.flip(t, axis=2)

    o_b, s_b = chunk_gated_delta(rev(q), rev(k), rev(v), rev(gb), rev(bb), s0[:, 1])
    o = jnp.swapaxes(o_f + rev(o_b), 1, 2)
    z = zc.astype(f32).reshape(Bn, L, N_HEADS_C, HEAD_DIM)
    o = rms_norm(o, norm_g) * jax.nn.silu(z)
    return o.reshape(Bn, L, GROUP_WIDTH).astype(qc.dtype), jnp.stack([s_f, s_b], axis=1)

def fourier_mix(xd):
    Bn, L, _ = xd.shape
    t = xd.astype(jnp.float32).reshape(Bn, L, N_FOURIER_GROUPS, FOURIER_GROUP_DIM)
    y = jnp.fft.fft2(t, axes=(1, 3), norm='ortho').real
    return y.reshape(Bn, L, GROUP_WIDTH).astype(xd.dtype)

def swiglu(h, w1, w3, w2):
    return (jax.nn.silu(h @ w1) * (h @ w3)) @ w2

def token_mix(h, lp, ctx):
    Bn, L, _ = h.shape
    (qa, ka, va, gate_b, gate_c, xb, qc, kc, vc, zc,
     beta_f, beta_b, a_f, a_b, xd) = split_cols(h @ lp['w_in'])
    qa = rms_norm(qa.reshape(Bn, L, N_HEADS_A, HEAD_DIM), lp['q_norm'])
    ka = rms_norm(ka.reshape(Bn, L, KV_HEADS_A, HEAD_DIM), lp['k_norm'])
    va = va.reshape(Bn, L, KV_HEADS_A, HEAD_DIM)
    if ctx is None:
        k_all, v_all = ka, va
        s0 = jnp.zeros((Bn, 2, N_HEADS_C, HEAD_DIM, HEAD_DIM), jnp.float32)
    else:
        k_ctx, v_ctx, s0 = ctx
        qa = rope_2d(qa)
        k_all = jnp.concatenate([jnp.swapaxes(k_ctx, 1, 2).astype(ka.dtype), rope_2d(ka)], axis=1)
        v_all = jnp.concatenate([jnp.swapaxes(v_ctx, 1, 2).astype(va.dtype), va], axis=1)
    o_a = block_attention(qa.reshape(Bn, L, KV_HEADS_A, Q_PER_KV, HEAD_DIM), k_all, v_all)
    o_b = gate_b * depthwise_conv(gate_c * xb, lp['conv_b_w'])
    o_c, s_end = gated_deltanet(qc, kc, vc, zc, beta_f, beta_b, a_f, a_b, lp['conv_c_w'],
                                lp['delta_a_log'], lp['delta_dt_bias'], lp['delta_norm'], s0)
    o_d = fourier_mix(xd)
    out = jnp.concatenate([o_a, o_b, o_c, o_d], axis=-1) @ lp['w_out']
    return out, jnp.swapaxes(ka, 1, 2), jnp.swapaxes(va, 1, 2), s_end.astype(h.dtype)

def trunk_layer(x, cond, lp, ctx):
    mod = (jax.nn.silu(cond) @ lp['mod_w'] + lp['mod_b'])[:, None, :]
    sh1, sc1, g1, shm, scm, gm, sh2, sc2, g2 = jnp.split(mod, N_MOD, axis=-1)
    h = rms_norm(x, lp['norm_ffn1']) * (1.0 + sc1) + sh1
    x = x + 0.5 * g1 * swiglu(h, lp['ffn1_w1'], lp['ffn1_w3'], lp['ffn1_w2'])
    h = rms_norm(x, lp['norm_mix']) * (1.0 + scm) + shm
    out, k_new, v_new, s_new = token_mix(h, lp, ctx)
    x = x + gm * out
    h = rms_norm(x, lp['norm_ffn2']) * (1.0 + sc2) + sh2
    x = x + 0.5 * g2 * swiglu(h, lp['ffn2_w1'], lp['ffn2_w3'], lp['ffn2_w2'])
    return x, k_new, v_new, s_new

def setup_inputs(seed: int = 0) -> dict:
    key = jax.random.key(seed)
    ks = jax.random.split(key, 32)
    f32 = jnp.float32

    def nrm(k, shape, scale):
        return jax.random.normal(k, shape, f32) * scale

    def gain(k, shape):
        return 1.0 + 0.02 * jax.random.normal(k, shape, f32)

    dt = jnp.exp(jax.random.uniform(ks[25], (DEPTH, 2, N_HEADS_C), f32,
                                    math.log(1e-3), math.log(0.1)))
    return {
        'x_prompt': nrm(ks[0], (BATCH, SEQ, D_MODEL), 1.0),
        'x_sample': nrm(ks[1], (DEC_BATCH, DEC_SEQ, D_MODEL), 1.0),
        'c': nrm(ks[2], (DEC_BATCH, D_MODEL), 1.0),
        'cache_k': nrm(ks[3], (DEC_BATCH, DEPTH, KV_HEADS_A, PAST_LEN, HEAD_DIM), 1.0),
        'cache_v': nrm(ks[4], (DEC_BATCH, DEPTH, KV_HEADS_A, PAST_LEN, HEAD_DIM), 1.0),
        'state_delta': nrm(ks[5], (DEC_BATCH, DEPTH, 2, N_HEADS_C, HEAD_DIM, HEAD_DIM), 0.1),
        'c_ctx': nrm(ks[6], (D_MODEL,), 1.0),
        'mod_w': nrm(ks[7], (DEPTH, D_MODEL, N_MOD * D_MODEL), D_MODEL ** -0.5),
        'mod_b': nrm(ks[8], (DEPTH, N_MOD * D_MODEL), 0.02),
        'norm_ffn1': gain(ks[9], (DEPTH, D_MODEL)),
        'norm_mix': gain(ks[10], (DEPTH, D_MODEL)),
        'norm_ffn2': gain(ks[11], (DEPTH, D_MODEL)),
        'ffn1_w1': nrm(ks[12], (DEPTH, D_MODEL, D_FF), D_MODEL ** -0.5),
        'ffn1_w3': nrm(ks[13], (DEPTH, D_MODEL, D_FF), D_MODEL ** -0.5),
        'ffn1_w2': nrm(ks[14], (DEPTH, D_FF, D_MODEL), D_FF ** -0.5),
        'ffn2_w1': nrm(ks[15], (DEPTH, D_MODEL, D_FF), D_MODEL ** -0.5),
        'ffn2_w3': nrm(ks[16], (DEPTH, D_MODEL, D_FF), D_MODEL ** -0.5),
        'ffn2_w2': nrm(ks[17], (DEPTH, D_FF, D_MODEL), D_FF ** -0.5),
        'w_in': nrm(ks[18], (DEPTH, D_MODEL, PROJ_WIDTH), D_MODEL ** -0.5),
        'w_out': nrm(ks[19], (DEPTH, MIX_WIDTH, D_MODEL), MIX_WIDTH ** -0.5),
        'q_norm': gain(ks[20], (DEPTH, HEAD_DIM)),
        'k_norm': gain(ks[21], (DEPTH, HEAD_DIM)),
        'conv_b_w': nrm(ks[22], (DEPTH, SHORT_CONV, GROUP_WIDTH), SHORT_CONV ** -0.5),
        'conv_c_w': nrm(ks[23], (DEPTH, SHORT_CONV, 3 * GROUP_WIDTH), SHORT_CONV ** -0.5),
        'delta_a_log': jnp.log(jax.random.uniform(ks[24], (DEPTH, 2, N_HEADS_C), f32, 1.0, 16.0)),
        'delta_dt_bias': dt + jnp.log(-jnp.expm1(-dt)),
        'delta_norm': gain(ks[26], (DEPTH, HEAD_DIM)),
        'final_norm': gain(ks[27], (D_MODEL,)),
    }

def reference(x_prompt, x_sample, c, cache_k, cache_v, state_delta, c_ctx,
              mod_w, mod_b, norm_ffn1, norm_mix, norm_ffn2,
              ffn1_w1, ffn1_w3, ffn1_w2, ffn2_w1, ffn2_w3, ffn2_w2,
              w_in, w_out, q_norm, k_norm, conv_b_w, conv_c_w,
              delta_a_log, delta_dt_bias, delta_norm, final_norm):
    yp = x_prompt
    ys = x_sample
    cond_ctx = c_ctx[None, :]
    k_list, v_list, s_list = [], [], []
    for l in range(DEPTH):
        lp = {
            'mod_w': mod_w[l], 'mod_b': mod_b[l],
            'norm_ffn1': norm_ffn1[l], 'norm_mix': norm_mix[l], 'norm_ffn2': norm_ffn2[l],
            'ffn1_w1': ffn1_w1[l], 'ffn1_w3': ffn1_w3[l], 'ffn1_w2': ffn1_w2[l],
            'ffn2_w1': ffn2_w1[l], 'ffn2_w3': ffn2_w3[l], 'ffn2_w2': ffn2_w2[l],
            'w_in': w_in[l], 'w_out': w_out[l], 'q_norm': q_norm[l], 'k_norm': k_norm[l],
            'conv_b_w': conv_b_w[l], 'conv_c_w': conv_c_w[l],
            'delta_a_log': delta_a_log[l], 'delta_dt_bias': delta_dt_bias[l],
            'delta_norm': delta_norm[l],
        }
        yp, k_l, v_l, s_l = trunk_layer(yp, cond_ctx, lp, None)
        k_list.append(k_l)
        v_list.append(v_l)
        s_list.append(s_l)
        ys, _, _, _ = trunk_layer(ys, c, lp, (cache_k[:, l], cache_v[:, l], state_delta[:, l]))
    y_prompt = rms_norm(yp, final_norm)
    y_sample = rms_norm(ys, final_norm)
    new_cache_k = jnp.stack(k_list, axis=1)
    new_cache_v = jnp.stack(v_list, axis=1)
    new_state_delta = jnp.stack(s_list, axis=1)
    return (y_prompt, y_sample, new_cache_k, new_cache_v, new_state_delta)


_drawn_inputs = setup_inputs


def setup_inputs(seed=0):
    import zlib

    import numpy as np

    out = dict(_drawn_inputs(seed))
    spreads = {}
    factors = {'cache_k': 4.942,
     'cache_v': 4.276,
     'norm_ffn1': 3.94,
     'norm_ffn2': 5.953,
     'q_norm': 33.438,
     'k_norm': 20.625,
     'delta_norm': 28.822,
     'final_norm': 29.081}
    for name, (base, spread) in spreads.items():
        noise = np.random.default_rng([zlib.crc32(name.encode()), seed]).standard_normal(out[name].shape)
        drawn = base * np.exp(spread * noise) if base else spread * noise
        out[name] = __import__('jax').numpy.asarray(drawn.astype(out[name].dtype))
    for name, factor in factors.items():
        out[name] = (out[name] * factor).astype(out[name].dtype)
    return out
```

```python
from contextlib import ExitStack

import concourse.bass as bass
from concourse import mybir

F32 = mybir.dt.float32
F32R = mybir.dt.float32r
ALU = mybir.AluOpType
ACT = mybir.ActivationFunctionType
AX = mybir.AxisListType

P = 128
D = 1024
KC = D // P
DEPTH = 2
CTX, LAT = 128, 512
T = CTX + LAT
NT = T // P
FF = 2816
HEAD = 64
PROJ = 2576
NMOD = 9
MODC = NMOD * KC
EPS = 1e-6
BLK = 256
NB_FF = FF // BLK
NB_MOD = NMOD * D // BLK
STREAMS = ((0, 0, CTX), (1, CTX, T))
HALVES = ((0, 320), (320, 640))

V_MODB, V_NORM, V_CONVB, V_CONVC, V_QN, V_KN, V_DN = 0, MODC, MODC + 24, MODC + 30, MODC + 48, MODC + 49, MODC + 50
V_ROWS = MODC + 51

C_QA, C_KA, C_VA, C_GB, C_GC, C_XB, C_QC, C_KC, C_VC, C_ZC, C_XD = 0, 2, 3, 4, 6, 8, 10, 12, 14, 16, 18
COL_ROWS = 2304
COL_XD = 2320
LEVELS = 7
NORMS = (C_QA, C_QA + 1, C_KA, C_KC, C_KC + 1, C_QC, C_QC + 1)

T_ID, T_ONE, T_MASK, T_NEG, T_TRI, T_SUM, T_BC, T_ROT = 0, 128, 256, 256 + 2 * LEVELS * 128, 0, 0, 0, 0
T_TRI = T_NEG + 256
T_SUM = T_TRI + 256
T_BC = T_SUM + 98
T_ROT = T_BC + 7 * 128
T_SC = T_ROT + 128
T_ALL = T_SC + 2
U_COS, U_SIN, U_DFT, U_CL, U_SL, U_CC, U_SCX = 0, 512, 1024, 1280, 1280 + 2048, 1280 + 4096, 1280 + 4096 + 128
U_ALL = U_SCX + 128

RAW_MOD, RAW_FF1, RAW_MIX, RAW_FF2, RAW_LAYER = 0, 12, 23, 28, 39
UN_FF1, UN_MIX = 0, 11


def un_ff2(u):
    return 15 if u == 3 else 16


def un_layer(u):
    return un_ff2(u) + NB_FF


OUT_BLOCKS = (1, 1, 2)

ACC_FF1, ACC_PROJ, ACC_OUT, ACC_FF2, ACC_LAYER = 0, 88, 110, 118, 206


class Event:

    def __init__(self, sem, per_layer, credit=0):
        self.sem, self.per_layer, self.credit = sem, per_layer, credit

    def at(self, layer, n):
        return layer * self.per_layer + (n + self.credit)


def build(nc, a, tables, mixer_tables, outs):
    with ExitStack() as ctx:
        ps_all = ctx.enter_context(nc.psum_tensor("ps", [P, 4096], F32))

        place = [((int(nc.sbuf_base) + 63) // 64) * 64]
        made = {}

        def at(name, cols, dt=F32, offset=None):
            off = place[0] if offset is None else offset
            t = nc.alloc_sbuf_tensor_at(name, [P, cols], dt, offset=off)
            if offset is None:
                place[0] = off + (cols * 4 + 31) // 32 * 32
            made[name] = off
            return t

        xT = at("xT", KC * T)[:].rearrange("p (c t) -> p c t", c=KC)
        hh = at("hh", KC * T, F32R)[:].rearrange("p (c t) -> p c t", c=KC)
        hl = at("hl", KC * T, F32R)[:].rearrange("p (c t) -> p c t", c=KC)
        raw = [at(f"raw{s}", 2048)[:] for s in range(3)]
        un = [(at(f"uh{u}", 1024, F32R)[:], at(f"ul{u}", 1024, F32R)[:]) for u in range(6)]
        arena0 = made["uh0"]
        PTt = at("PT", 21 * T)
        PT = PTt[:].rearrange("p (c t) -> p c t", c=21)
        pt0 = made["PT"]
        gh = at("gh", 4 * T, F32R, pt0)[:].rearrange("p (g t) -> p g t", g=4)
        gl = at("gl", 4 * T, F32R, pt0 + 4 * T * 4)[:].rearrange("p (g t) -> p g t", g=4)
        PS = PT[:, 20, :]
        tb = at("tb", T_ALL)[:]
        vrow = at("vrow", 128)[:]
        vcol = at("vcol", 128)[:]
        condT = at("condT", 16)[:].rearrange("p (s k) -> p k s", s=2)
        condE = at("condE", 16)[:]
        fcol = at("fcol", 8)[:]
        modT = at("modT", MODC * 2)[:].rearrange("p (c s) -> p c s", s=2)
        mA = at("mA", 48)[:].rearrange("p (n c s) -> p n c s", n=3, c=KC)
        nst = at("nst", 16)[:]
        ast = at("ast", 16)[:]
        gsm = at("gsm", 400)[:]
        adt = at("adt", 4)[:]
        assert place[0] <= int(nc.sbuf_usable_end), (place[0], nc.sbuf_usable_end)

        def ar(name, off, cols):
            assert off + cols <= 12288
            return at(name, cols, F32, arena0 + 4 * off)[:]

        ub = ar("ub", 0, U_ALL)
        A0 = U_ALL
        sq7 = ar("sq7", A0, 7 * T + 0)[:, 0:7 * T].rearrange("p (c t) -> p c t", c=7) if A0 + 7 * T <= 12288 else None
        cv = ar("cv", A0 + 7 * T, 2 * T).rearrange("p (b t) -> p b t", b=2)
        rrow = cv
        xcs = ar("xcs", A0, 5 * 256).rearrange("p (t n) -> p t n", t=5)
        kall = ar("kall", A0 + 1280, T)
        vtok = ar("vtok", A0 + 1920, 6 * 128).rearrange("p (t n) -> p t n", t=6)
        pexp = ar("pexp", A0 + 2688, 2 * T).rearrange("p (b t) -> p b t", b=2)
        pTs = ar("pTs", A0 + 3968, T).rearrange("p (k n) -> p k n", k=5)
        qs = ar("qs", A0 + 4608, 256).rearrange("p (c t) -> p c t", c=2)
        ckr = ar("ckr", A0 + 4864, 128)
        kct = ar("kct", A0 + 4992, 128)
        rtmp = ar("rtmp", A0 + 5120, 512)
        def dn(name, off, d, cols):
            return ar(f"{name}{d}", d * 6144 + off, cols)
        dd = []
        for d in range(2):
            f4 = lambda n, o: dn(n, o, d, 512).rearrange("p (h t) -> p h t", h=4)
            f2 = lambda n, o: dn(n, o, d, 256).rearrange("p (c t) -> p c t", c=2)
            dd.append(dict(E=f4("dE", 0), AQ=f4("dAQ", 512), LT=f4("dLT", 1024), B0=f4("dB0", 1536), B1=f4("dB1", 2048),
                           Y=f4("dY", 2560), T=f4("dT", 3072), TT=f4("dTT", 3584), kbg=f2("dkbg", 4096), vb=f2("dvb", 4352),
                           kdec=f2("dkdec", 4608), nwT=f2("dnwT", 4864), vnew=f2("dvnew", 5120), qg=f2("dqg", 5376),
                           kbT=f2("dkbT", 5632), kst=f2("dkst", 5888)))
            dd[d]["qst"] = f2("dqst", 2048)

        oC = PT[:, 0:2, :]
        ktok = PT[:, 4:6, :].rearrange("p c (t n) -> p c t n", t=NT)
        vtokc = PT[:, 6:8, :].rearrange("p c (t n) -> p c t n", t=NT)
        gcr = PT[0:8, 8, :]
        er = PT[0:8, 9, :]
        Sctx = PT[:, 2, 0:512].rearrange("p (d c n) -> p d c n", d=2, c=2)
        Slat = PT[:, 3, 0:512].rearrange("p (d c n) -> p d c n", d=2, c=2)
        sq8 = PT[:, 12:20, :]
        t1 = PT[:, 8:10, :]
        diag = PT[:, 10, :].rearrange("p (t n) -> p t n", t=NT)
        sil = PT[:, 8:10, :]
        gf = PT[:, 10:12, :]

        gk = lambda i: gsm[:, 40 * i:40 * i + 40].rearrange("p (t e) -> p t e", t=NT)
        G_BETA, G_G, G_GC, G_EG, G_BG, G_KD, G_EGL, G_T = range(8)

        def tcol(c, n=128):
            return tb[:, c:c + n]
        ident, ones = tcol(T_ID), tcol(T_ONE)
        mask = lambda d, lv: tcol(T_MASK + (d * LEVELS + lv) * 128)
        negm = lambda d: tcol(T_NEG + 128 * d)
        tri = lambda d: tcol(T_TRI + 128 * d)

        def bank(b, n=512, at=0):
            return ps_all[:, b * 512 + at:b * 512 + at + n]

        def pair(q):
            return ps_all[:, q * 1024 + 192:q * 1024 + 832]

        def tiles5(b):
            return ps_all[:, b * 512 + 384:b * 512 + 1024].rearrange("p (t n) -> p t n", t=5)

        def S(name):
            return ctx.enter_context(nc.semaphore(name))

        def ev(name, per_layer, credit=0):
            return Event(S(name), per_layer, credit)

        raw_full = [S(f"raw_full{s}") for s in range(3)]
        raw_free = [ev(f"raw_free{s}", RAW_LAYER, 1) for s in range(3)]
        hi_done = [ev(f"hi_done{u}", un_layer(u)) for u in range(6)]
        split_full = [ev(f"split_full{u}", un_layer(u)) for u in range(6)]
        unit_done = [ev(f"unit_done{u}", un_layer(u), 1) for u in range(6)]
        acc_used = ev("acc_used", ACC_LAYER, 2)
        y_done = ev("y_done", 14 * NB_FF)
        tables_in, x_in, vec_in, out_done, st_in = S("tables_in"), S("x_in"), S("vec_in"), S("out_done"), S("st_in")
        xt_done, xt_used, cond_done, cond_exp, cond_ready = S("xt_done"), S("xt_used"), S("cond_done"), S("cond_exp"), S("cond_ready")
        vec_zero, settled = S("vec_zero"), S("settled")
        vecT_done, vec_ready, x_ready = ev("vecT_done", 1), ev("vec_ready", 1), ev("x_ready", 3)
        sq_ready, ss_done, ms_ready, rt_ready, diag_ready = (ev(n, 3) for n in ("sq_ready", "ss_done", "ms_ready", "rt_ready", "diag_ready"))
        rb_done = ev("rb_done", 3)
        t1_ready, hh_ready, h_ready = ev("t1_ready", 24), ev("hh_ready", 24), ev("h_ready", 24)
        sil_ready, gf_ready, gh_ready, g_ready = (ev(n, 4 * NB_FF) for n in ("sil_ready", "gf_ready", "gh_ready", "g_ready"))
        proj_done = ev("proj_done", 1)
        mt_in = ev("mt_in", 16 * 5)
        cv_ready, cv_used = ev("cv_ready", 6), ev("cv_used", 6)
        ob_ready, ob_hi = ev("ob_ready", 1), ev("ob_hi", 1)
        sq7_ready, nr_done, nq_ready, nrow_ready = (ev(n, 2) for n in ("sq7_ready", "nr_done", "nq_ready", "nrow_ready"))
        bc_done, bc_used = ev("bc_done", 9), ev("bc_used", 9)
        tr_done, tr_used, rot_done, roped = ev("tr_done", 1), ev("tr_used", 1), ev("rot_done", 3), ev("roped", 1)
        qs_ready = ev("qs_ready", 5)
        s_done, nmax_ready, p_exp, p_ready, pT_done, pT_used, pv_done = (ev(n, 20) for n in ("s_done", "nmax_ready", "p_exp", "p_ready", "pT_done", "pT_used", "pv_done"))
        pv_used = ev("pv_used", 10)
        f1_done, f1_used, f2_done, f_hi, f_lo = (ev(n, 2) for n in ("f1_done", "f1_used", "f2_done", "f_hi", "f_lo"))
        e_rows, rows_ready, e_ln = ev("e_rows", 1), ev("rows_ready", 1), ev("e_ln", 1)
        sp_x = ev("sp_x", 1)
        gt_done, gt_used, gc_done, gc_ready, gexp_ready, gcol_ready = (ev(n, 1) for n in ("gt_done", "gt_used", "gc_done", "gc_ready", "gexp_ready", "gcol_ready"))
        gr_done, gr_used, kv_done, kv_used = ev("gr_done", 1), ev("gr_used", 1), ev("kv_done", 4), ev("kv_used", 4)
        oz_ready = ev("oz_ready", 1)
        dv = [dict((n, ev(f"{n}{d}", k * NT)) for n, k in (
            ("bcast", 1), ("diff", 1), ("decay", 1), ("staged", 1), ("gram", 1), ("lt", 1), ("bm", LEVELS), ("b1", 1), ("tt", LEVELS),
            ("y", LEVELS - 1), ("ye", LEVELS - 1), ("p1", LEVELS - 2), ("p2", LEVELS - 1), ("tk", LEVELS - 1), ("kb", 1),
            ("wt", 1), ("wte", 1), ("vn", 1), ("vne", 1), ("os", 1), ("ose", 1))) for d in range(2)]
        st_out = ev("st_out", 16 * 4)
        oc_ready, oc_gate, oc_hi, oc_lo = ev("oc_ready", 1), ev("oc_gate", 1), ev("oc_hi", 1), ev("oc_lo", 1)
        kv_out = ev("kv_out", 32)
        fin_sq, fin_ss, fin_ms, fin_rt, fin_x, fin_t, fin_e = (S(n) for n in ("fin_sq", "fin_ss", "fin_ms", "fin_rt", "fin_x", "fin_t", "fin_e"))

        block = ctx.enter_context(nc.Block())

        xrow = PTt[:, 0:NT * D].rearrange("p (t n) -> p t n", t=NT)
        fin_row = PTt[:, NT * D:2 * NT * D].rearrange("p (t n) -> p t n", t=NT)

        def raw_view(s, c, kind):
            if kind == "heads":
                return raw[s].rearrange("p (k g c n) -> p k g c n", k=KC, g=2, c=2)[:, :, :, c, :]
            if kind == "rows":
                return raw[s][:, c * 1024:(c + 1) * 1024]
            return raw[s].rearrange("p (k n) -> p k n", k=KC)[:, :, c * P:(c + 1) * P]

        def settle(eng):
            eng.sem_inc(settled, 1)

        def raw_count(l, s, use, extra=0):
            return l * (32 * RAW_LAYER + 16 * OUT_BLOCKS[s]) + (32 * (use + 1) + 16 * extra)

        def un_view(u, kind):
            if kind == "heads":
                return u.rearrange("p (k g n) -> p k g n", k=KC, g=2)
            return u if kind == "rows" else u.rearrange("p (k n) -> p k n", k=KC)

        @block.sync
        def _(sp):
            sp.dma_start(tb, tables).then_inc(tables_in, 16)
            sp.dma_start(xrow[:, 0, :], a["x_prompt"][0]).then_inc(x_in, 16)
            sp.dma_start(xrow[:, 1:NT, :], a["x_sample"][0].rearrange("(t p) n -> p t n", p=P)).then_inc(x_in, 16)
            for s in range(3):
                sp.sem_inc(raw_free[s].sem, 1)

            def load(l, s, use, first, second):
                sp.wait_ge(raw_free[s].sem, raw_free[s].at(l, use))
                for dst, src in (first, second):
                    sp.dma_start(dst, src).then_inc(raw_full[s], 16)

            def load_cols(l, s, use, w, col):
                r = raw[s].rearrange("p (k n) -> p k n", k=KC)
                v = w.rearrange("(k p) n -> p k n", p=P)[:, :, bass.ds(col, BLK)]
                load(l, s, use, (r[:, 0:4, :], v[:, 0:4, :]), (r[:, 4:8, :], v[:, 4:8, :]))

            def feed_forward(l, w1, w3, w2, base):
                with sp.Fori(0, NB_FF) as i:
                    load_cols(l, 0, base + i, w1, i * BLK)
                    load_cols(l, 1, base + i, w3, i * BLK)
                    r = raw[2].rearrange("p (k n) -> p k n", k=2)
                    v = w2[bass.ds(i * BLK, BLK), :].rearrange("(k p) n -> p k n", p=P)
                    load(l, 2, base + i, (r[:, 0, :], v[:, 0, :]), (r[:, 1, :], v[:, 1, :]))

            with sp.Fori(0, DEPTH) as l:
                def w(name):
                    return a[name][bass.ds(l, 1)].rearrange("o k n -> (o k) n")
                with sp.Fori(0, NB_MOD // 3) as i:
                    for s in range(3):
                        load_cols(l, s, RAW_MOD + i, w("mod_w"), (3 * i + s) * BLK)
                feed_forward(l, w("ffn1_w1"), w("ffn1_w3"), w("ffn1_w2"), RAW_FF1)
                win = w("w_in")
                for j in range(10):
                    s, use = j % 3, RAW_MIX + j // 3
                    load_cols(l, s, use, win, COL_XD if j == 9 else j * BLK)
                r = raw[1].rearrange("p (k n) -> p k n", k=KC)
                v = win.rearrange("(k p) n -> p k n", p=P)
                load(l, 1, RAW_MIX + 3, (r[:, :, 0:8], v[:, :, COL_ROWS:COL_ROWS + 8]),
                     (r[:, :, 32:40], v[:, :, COL_ROWS + 8:COL_ROWS + 16]))
                wout = w("w_out")
                for j in range(4):
                    s = (2, 0, 1, 2)[j]
                    use = RAW_MIX + (3, 4, 4, 4)[j]
                    r = raw[s].rearrange("p (k n) -> p k n", k=KC)
                    cols = wout[:, j * BLK:(j + 1) * BLK]
                    sp.wait_ge(raw_free[s].sem, raw_free[s].at(l, use))
                    for c in range(2):
                        sp.dma_start(r[:, c, :], cols[0:256, :].rearrange("(g c q) n -> c g q n", g=2, c=2)[c]).then_inc(raw_full[s], 16)
                    sp.dma_start(r[:, 2:8, :], cols.rearrange("(k p) n -> p k n", p=P)[:, 2:8, :]).then_inc(raw_full[s], 16)
                feed_forward(l, w("ffn2_w1"), w("ffn2_w3"), w("ffn2_w2"), RAW_FF2)

            sp.wait_ge(fin_e, 2)
            sp.dma_start(outs[0][0], fin_row[:, 0, :]).then_inc(out_done, 16)
            for t in range(1, NT):
                sp.wait_ge(fin_e, 2 * t + 2)
                sp.dma_start(outs[1][0, (t - 1) * P:t * P, :], fin_row[:, t, :]).then_inc(out_done, 16)
            sp.wait_ge(out_done, 16 * NT)

        @block.gpsimd
        def _(pool):
            pool.memset(vrow, 0.0)
            pool.drain().then_inc(vec_zero, 1)
            pool.wait_ge(vec_zero, 1)
            pool.dma_start(vrow[0:8, :], a["c_ctx"].rearrange("(k p) -> k p", p=P)).then_inc(st_in, 16)
            pool.dma_start(vrow[8:16, :], a["c"][0].rearrange("(k p) -> k p", p=P)).then_inc(st_in, 16)
            pool.dma_start(vrow[16:24, :], a["final_norm"].rearrange("(k p) -> k p", p=P)).then_inc(st_in, 16)
            pool.wait_ge(cond_ready, 1)
            with pool.Fori(0, DEPTH) as l:
                one = bass.ds(l, 1)

                def vec(row, n, src):
                    pool.dma_start(vrow[row:row + n, :], src).then_inc(vec_in, 16)
                vecT_done_prev = l * 1 + 1
                pool.wait_ge(cond_ready, vecT_done_prev)
                vec(V_MODB, MODC, a["mod_b"][one].rearrange("o (k p) -> (o k) p", p=P))
                for n, name in enumerate(("norm_ffn1", "norm_mix", "norm_ffn2")):
                    vec(V_NORM + 8 * n, 8, a[name][one].rearrange("o (k p) -> (o k) p", p=P))
                vec(V_CONVB, 6, a["conv_b_w"][one].rearrange("o j (k p) -> (o j k) p", p=P))
                vec(V_CONVC, 18, a["conv_c_w"][one].rearrange("o j (k p) -> (o j k) p", p=P))
                for v, name in ((V_QN, "q_norm"), (V_KN, "k_norm"), (V_DN, "delta_norm")):
                    for g in range(2):
                        pool.dma_start(vrow[v:v + 1, g * HEAD:(g + 1) * HEAD], a[name][one]).then_inc(vec_in, 16)

                pool.wait_ge(proj_done.sem, proj_done.at(l, 1))
                settle(pool)
                pool.dma_start(ub, mixer_tables).then_inc(mt_in.sem, 16)
                for g, name in enumerate(("delta_a_log", "delta_dt_bias")):
                    pool.dma_start(adt[32:40, g:g + 1], a[name][one].rearrange("o d (h u) -> (o d h) u", u=1)).then_inc(mt_in.sem, 16)
                pool.wait_ge(bc_used.sem, bc_used.at(l, 7))
                settle(pool)
                pool.dma_start(ckr.rearrange("p (h n) -> p h n", h=2),
                               a["cache_k"][0, one].rearrange("o h t n -> (o t) h n")).then_inc(mt_in.sem, 16)
                pool.dma_start(vtok[:, 0, :].rearrange("p (h n) -> p h n", h=2),
                               a["cache_v"][0, one].rearrange("o h t n -> (o t) h n")).then_inc(mt_in.sem, 16)
                pool.wait_ge(tr_used.sem, tr_used.at(l, 1))
                settle(pool)
                pool.dma_start(outs[2][0, one].rearrange("o h t n -> (o t) h n"),
                               kct.rearrange("p (h n) -> p h n", h=2)).then_inc(kv_out.sem, 16)
                pool.dma_start(outs[3][0, one].rearrange("o h t n -> (o t) h n"),
                               vtok[:, 5, :].rearrange("p (h n) -> p h n", h=2)).then_inc(kv_out.sem, 16)
                pool.wait_ge(kv_out.sem, kv_out.at(l, 32))
                pool.wait_ge(pv_done.sem, pv_done.at(l, 20))
                pool.wait_ge(roped.sem, roped.at(l, 1))
                settle(pool)
                pool.memset(PT[:, 2:4, 0:512], 0.0)
                pool.memset(oC, 0.0)
                pool.drain().then_inc(oz_ready.sem, 1)
                pool.wait_ge(oz_ready.sem, oz_ready.at(l, 1))
                settle(pool)
                for c in range(2):
                    for g in range(2):
                        pool.dma_start(Slat[64 * g:64 * g + 64, :, c, 64 * g:64 * g + 64],
                                       a["state_delta"][0, one, :, 2 * c + g].rearrange("o d k v -> (o k) d v")).then_inc(st_in, 16)

                def tile(n):
                    for lv in range(LEVELS):
                        for d in range(2):
                            b, e = dd[d], dv[d]
                            if lv == 0:
                                pool.wait_ge(e["lt"].sem, e["lt"].at(l, n + 1))
                            if lv >= 3:
                                pool.wait_ge(e["y"].sem, e["y"].at(l, (LEVELS - 1) * n + lv - 2))
                            if lv == 2:
                                pool.wait_ge(e["tt"].sem, e["tt"].at(l, LEVELS * n + 1))
                            pool.tensor_tensor(b["B0" if lv % 2 == 0 else "B1"], b["LT"],
                                               mask(d, lv).rearrange("p (o n) -> p o n", o=1).to_broadcast([P, 4, 128]),
                                               ALU.mult).then_inc(e["bm"].sem, 1)
                tile(0)
                for d in range(2):
                    pool.wait_ge(dv[d]["ose"].sem, dv[d]["ose"].at(l, 1))
                settle(pool)
                for c in range(2):
                    for g in range(2):
                        pool.dma_start(outs[4][0, one, :, 2 * c + g].rearrange("o d k v -> (o k) d v"),
                                       Sctx[64 * g:64 * g + 64, :, c, 64 * g:64 * g + 64]).then_inc(st_out.sem, 16)
                with pool.Fori(1, NT) as i:
                    tile(i)
                pool.wait_ge(st_out.sem, st_out.at(l, 64))

        @block.tensor
        def _(pe):
            def fp32(out, lhsT, rhs, start=True, stop=True, loose=False):
                return pe.matmul(out, lhsT, rhs, start=start, stop=stop, skip_group_check=loose)

            def chunk_product(q, u, ks, first_k=None, start=True, stop=True, rhs=None, wait_k=None):
                wh, wl = un[u]
                last = None
                n = len(ks)
                for i, (wk, mk) in enumerate(ks):
                    if wait_k:
                        wait_k(mk)
                    mh, ml = rhs
                    for p_, (wt, mv) in enumerate(((wh, mh), (wh, ml), (wl, mh))):
                        for lo, hi in HALVES:
                            last = pe.matmul(pair(q)[:, lo:hi], wt[:, wk * P:(wk + 1) * P], mv(mk, lo, hi),
                                             start=start and i == 0 and p_ == 0, stop=stop and i == n - 1 and p_ == 2)
                return last

            h_rhs = (lambda k, lo, hi: hh[:, k, lo:hi], lambda k, lo, hi: hl[:, k, lo:hi])
            k8 = [(k, k) for k in range(KC)]

            def norm(l, st):
                pe.wait_ge(sq_ready.sem, sq_ready.at(l, st + 1))
                for t in range(NT):
                    for c in range(KC):
                        mm = fp32(bank(4, 1, t), sq8[:, c, t * P:(t + 1) * P], ones[:, 0:1], c == 0, c == KC - 1)
                mm.then_inc(ss_done.sem, 1)
                pe.wait_ge(diag_ready.sem, diag_ready.at(l, st + 1))
                for t in range(NT):
                    mm = fp32(tiles5(5)[:, t, :], ones, diag[:, t, :])
                mm.then_inc(rb_done.sem, 1)

            def feed_forward(l, f):
                ubase = [0] * 6 if f == 0 else [un_ff2(u) for u in range(6)]
                st = 0 if f == 0 else 2
                abase = ACC_FF1 if f == 0 else ACC_FF2

                def up(i, first=False):
                    for c in range(2):
                        for w in range(2):
                            u = 2 * w + c
                            pe.wait_ge(split_full[u].sem, split_full[u].at(l, ubase[u] + i + 1))
                            n = 2 * NB_FF * f + 2 * i + c
                            ev_ = sil_ready if w == 0 else gf_ready
                            if not (first and c == 0):
                                pe.wait_ge(ev_.sem, ev_.at(l, n))
                            wk = (lambda k: pe.wait_ge(h_ready.sem, h_ready.at(l, 8 * st + k + 1))) if first and c == 0 and w == 0 else None
                            chunk_product(w, u, k8, rhs=h_rhs, wait_k=wk).then_inc(unit_done[u].sem, 1)

                def down(i):
                    par = 2 * (i % 2)
                    for g in range(2):
                        pe.wait_ge(g_ready.sem, g_ready.at(l, 2 * NB_FF * f + 2 * i + g + 1))
                        pe.wait_ge(split_full[4 + g].sem, split_full[4 + g].at(l, ubase[4 + g] + i + 1))
                    for o in range(KC):
                        pe.wait_ge(acc_used.sem, acc_used.at(l, abase + 8 * i + o - 1))
                        for g in range(2):
                            rhs = (lambda k, lo, hi: gh[:, bass.ds(par + k, 1), lo:hi].rearrange("p o t -> p (o t)"),
                                   lambda k, lo, hi: gl[:, bass.ds(par + k, 1), lo:hi].rearrange("p o t -> p (o t)"))
                            mm = chunk_product(2 + o % 2, 4 + g, [(o, g)], start=g == 0, stop=g == 1, rhs=rhs)
                            if o == KC - 1:
                                mm.then_inc(unit_done[4 + g].sem, 1)
                        if o < KC - 1:
                            mm.then_inc(y_done.sem, 1)
                norm(l, st)
                up(0, True)
                with pe.Fori(1, NB_FF) as i:
                    up(i)
                    down(i - 1)
                down(NB_FF - 1)

            pe.wait_ge(tables_in, 16)
            pe.wait_ge(x_in, 32)
            n = 0
            for t in range(NT):
                for q in range(2):
                    b = n % 4
                    if n >= 4:
                        pe.wait_ge(xt_used, n - 3)
                    for c in range(4):
                        mm = pe.transpose(bank(b, 128, c * 128), xrow[:, t, (4 * q + c) * P:(4 * q + c + 1) * P], ident)
                    mm.then_inc(xt_done, 1)
                    n += 1
            pe.wait_ge(st_in, 48)
            pe.transpose(bank(4, 128), vrow, ident).then_inc(cond_done, 1)
            pe.wait_ge(cond_ready, 1)
            for u in range(6):
                pe.sem_inc(unit_done[u].sem, 1)

            with pe.Fori(0, DEPTH) as l:
                pe.wait_ge(vec_in, 16 * 12 * (l + 1))
                pe.wait_ge(acc_used.sem, acc_used.at(l, 0))
                pe.transpose(bank(6, 128), vrow, ident).then_inc(vecT_done.sem, 1)
                with pe.Fori(0, NB_MOD // 3) as i:
                    for s in range(3):
                        pe.wait_ge(raw_full[s], raw_count(l, s, RAW_MOD + i))
                        r = raw[s].rearrange("p (k n) -> p k n", k=KC)
                        for c in range(2):
                            for k in range(KC):
                                mm = fp32(ps_all[:, bass.ds(7 * 512 + i * 12 + (4 * s + 2 * c), 2)],
                                          r[:, k, c * P:(c + 1) * P], condT[:, k, :], k == 0, k == KC - 1)
                        mm.then_inc(raw_free[s].sem, 1)
                feed_forward(l, 0)

                norm(l, 1)

                def project(q, s, c, use, first=False):
                    u = 2 * s + c
                    pe.wait_ge(split_full[u].sem, split_full[u].at(l, UN_MIX + use + 1))
                    pe.wait_ge(acc_used.sem, acc_used.at(l, ACC_PROJ + q - 1))
                    chunk_product(2 + q % 2 if isinstance(q, int) else 2 + c, u, k8, rhs=h_rhs,
                                  wait_k=(lambda k: pe.wait_ge(h_ready.sem, h_ready.at(l, 8 + k + 1))) if first else None).then_inc(unit_done[u].sem, 1)
                pe.wait_ge(h_ready.sem, h_ready.at(l, 16))
                settle(pe)
                with pe.Fori(0, 3) as i:
                    for s in range(3):
                        for c in range(2):
                            project(6 * i + (2 * s + c), s, c, i)
                for c in range(2):
                    project(18 + c, 0, c, 3)
                project(20, 1, 0, 3)

                def head_norm_rows(k, chunks):
                    pe.wait_ge(sq7_ready.sem, sq7_ready.at(l, k + 1))
                    for lo, hi in HALVES:
                        for c in range(chunks):
                            mm = fp32(pair(0)[0:14, lo:hi], tb[:, T_SUM + 14 * c:T_SUM + 14 * c + 14],
                                      (sq7 if k == 0 else PT[:, 4:6, :])[:, c, lo:hi], c == 0, c == chunks - 1)
                    mm.then_inc(nr_done.sem, 1)

                def head_norm_spread(k, chunks):
                    pe.wait_ge(nrow_ready.sem, nrow_ready.at(l, k + 1))
                    for c in range(chunks):
                        n = 7 * k + c
                        if c >= 2:
                            pe.wait_ge(bc_used.sem, bc_used.at(l, n - 1))
                        for lo, hi in HALVES:
                            mm = fp32(pair(1 + c % 2)[:, lo:hi], tb[0:14, T_BC + 128 * c:T_BC + 128 * c + 128],
                                      rrow[0:14, 0, lo:hi] if k == 0 else PT[0:14, 8, lo:hi])
                        mm.then_inc(bc_done.sem, 1)
                pe.wait_ge(proj_done.sem, proj_done.at(l, 1))
                head_norm_rows(0, 7)
                head_norm_spread(0, 7)

                pe.wait_ge(bc_used.sem, bc_used.at(l, 7))
                pe.wait_ge(mt_in.sem, mt_in.at(l, 80))
                for t in range(1, NT):
                    pe.transpose(bank(0, 128, (t - 1) * 128), PT[:, C_VA, t * P:(t + 1) * P], ident)
                pe.transpose(bank(1, 128, 0), PT[:, C_VA, 0:P], ident)
                pe.transpose(bank(1, 128, 128), PT[:, C_KA, 0:P], ident)
                pe.transpose(bank(1, 128, 256), ckr, ident).then_inc(tr_done.sem, 1)
                for n, c in enumerate((C_QA, C_QA + 1, C_KA)):
                    fp32(bank(2 + n), tcol(T_ROT), PT[:, c, CTX:T]).then_inc(rot_done.sem, 1)
                pe.wait_ge(roped.sem, roped.at(l, 1))
                pe.wait_ge(tr_used.sem, tr_used.at(l, 1))

                def attend(n, latent):
                    pe.wait_ge(qs_ready.sem, qs_ready.at(l, n + 1))

                    def scores(k):
                        c, g = k // 2, k % 2
                        if k >= 2:
                            pe.wait_ge(p_exp.sem, p_exp.at(l, 4 * n + k - 1))
                        lhs = qs[64 * g:64 * g + 64, c, :]
                        if latent:
                            for lo, hi in HALVES:
                                mm = fp32(pair(k % 2)[:, lo:hi], lhs, kall[64 * g:64 * g + 64, lo:hi])
                        else:
                            mm = fp32(pair(k % 2)[:, 0:P], lhs, PT[64 * g:64 * g + 64, C_KA, 0:P])
                        mm.then_inc(s_done.sem, 1)

                    def turn(k):
                        pe.wait_ge(p_ready.sem, p_ready.at(l, 4 * n + k + 1))
                        if k >= 1:
                            pe.wait_ge(pT_used.sem, pT_used.at(l, 4 * n + k))
                        for t in range(5 if latent else 1):
                            mm = pe.transpose(tiles5(4)[:, t, :], pexp[:, k % 2, t * P:(t + 1) * P], ident)
                        mm.then_inc(pT_done.sem, 1)

                    def values(k):
                        c, g = k // 2, k % 2
                        pe.wait_ge(pT_used.sem, pT_used.at(l, 4 * n + k + 1))
                        if latent and g == 0:
                            pe.wait_ge(pv_used.sem, pv_used.at(l, 2 * n + c - 1))
                        for t in range(5 if latent else 1):
                            mm = fp32(ps_all[64 * g:64 * g + 64, (6 + c) * 512:(6 + c) * 512 + 128],
                                      vtok[:, t if latent else 5, 64 * g:64 * g + 64], pTs[:, t, :], t == 0, t == (4 if latent else 0))
                        mm.then_inc(pv_done.sem, 1)
                    scores(0)
                    scores(1)
                    for k in range(4):
                        turn(k)
                        if k + 2 < 4:
                            scores(k + 2)
                        values(k)
                attend(0, False)
                with pe.Fori(1, NT) as i:
                    attend(i, True)

                pe.wait_ge(pv_used.sem, pv_used.at(l, 10))
                for c in range(2):
                    if c:
                        pe.wait_ge(f1_used.sem, f1_used.at(l, c))
                    for t in range(NT):
                        mm = fp32(ps_all[:, t * 256:(t + 1) * 256], PT[:, C_XD + c, t * P:(t + 1) * P], ub[:, U_DFT:U_DFT + 256])
                    mm.then_inc(f1_done.sem, 1)
                    pe.wait_ge(f1_used.sem, f1_used.at(l, c + 1))
                    if c:
                        pe.wait_ge(f_lo.sem, f_lo.at(l, c))
                    fp32(bank(4, 128, 384), xcs[:, 0, 0:128], ub[:, U_CC:U_CC + 128], True, False)
                    fp32(bank(4, 128, 384), xcs[:, 0, 128:256], ub[:, U_SCX:U_SCX + 128], False, True)
                    for t in range(1, NT):
                        for g in range(2):
                            u0 = (U_CL, U_SL)[g] + (t - 1) * 512
                            mm = fp32(bank(5), xcs[:, t, g * 128:(g + 1) * 128], ub[:, u0:u0 + 512], t == 1 and g == 0, t == NT - 1 and g == 1)
                    mm.then_inc(f2_done.sem, 1)

                pe.wait_ge(rows_ready.sem, rows_ready.at(l, 1))
                pe.wait_ge(f_lo.sem, f_lo.at(l, 2))
                settle(pe)
                for t in range(NT):
                    pe.transpose(bank(0, 8, 8 * t), PS[0:8, t * P:(t + 1) * P], ident[0:8, 0:8])
                for t in range(NT):
                    mm = pe.transpose(bank(2, 8, 8 * t), PS[32:40, t * P:(t + 1) * P], ident[32:40, 32:40])
                mm.then_inc(gt_done.sem, 1)
                for k, (chunk) in enumerate((C_KC, C_KC + 1, C_VC, C_VC + 1)):
                    if k >= 2:
                        pe.wait_ge(kv_used.sem, kv_used.at(l, k - 1))
                    for t in range(NT):
                        mm = pe.transpose(tiles5((4, 6)[k % 2])[:, t, :], PT[:, chunk, t * P:(t + 1) * P], ident)
                    mm.then_inc(kv_done.sem, 1)
                pe.wait_ge(gt_used.sem, gt_used.at(l, 1))
                for d in range(2):
                    fp32(bank(1, 40).rearrange("p (t d h) -> p t d h", t=NT, d=2)[:, :, d, :], tri(d), gk(G_G)[:, :, 4 * d:4 * d + 4])
                fp32(bank(1, 40, 40), ones, gk(G_G)).then_inc(gc_done.sem, 1)
                pe.wait_ge(gc_ready.sem, gc_ready.at(l, 1))
                for t in range(NT):
                    mm = pe.transpose(tiles5(2)[0:8, t, :], gk(G_GC)[:, t, :], ident)
                mm.then_inc(gr_done.sem, 1)
                pe.wait_ge(gr_used.sem, gr_used.at(l, 1))
                pe.wait_ge(gcol_ready.sem, gcol_ready.at(l, 1))
                pe.wait_ge(kv_used.sem, kv_used.at(l, 4))
                pe.wait_ge(oz_ready.sem, oz_ready.at(l, 1))
                pe.wait_ge(st_in, 48 + 64 * (l + 1))
                settle(pe)

                def delta(tiles, n, St):
                    cols = [bass.ds(t * P, P) for t in tiles]
                    h4 = lambda d, b: bank(4 * d + b).rearrange("p (h t) -> p h t", h=4)
                    h2 = lambda d, b: bank(4 * d + b, 256).rearrange("p (c t) -> p c t", c=2)
                    for d in range(2):
                        e = dv[d]
                        if not (isinstance(n, int) and n == 0):
                            pe.wait_ge(e["ose"].sem, e["ose"].at(l, n))
                            settle(pe)
                        for h in range(4):
                            r = 4 * d + h
                            fp32(h4(d, 0)[:, h, :], ident[0:8, r:r + 1].to_broadcast([8, P]), gcr[:, cols[d]])
                        for c in range(2):
                            sel = tb[0:8, T_BC + 128 * (2 * d + c):T_BC + 128 * (2 * d + c) + 128]
                            fp32(bank(4 * d + 1, 128, 128 * c), sel, er[:, cols[d]])
                            mm = fp32(bank(4 * d + 1, 128, 256 + 128 * c), sel, PS[0:8, cols[d]])
                        mm.then_inc(e["bcast"].sem, 1)
                    for d in range(2):
                        b, e = dd[d], dv[d]
                        pe.wait_ge(e["staged"].sem, e["staged"].at(l, n + 1))
                        for h in range(4):
                            g, c = 64 * (h % 2), h // 2
                            fp32(bank(4 * d + 2 + h % 2, P, c * P), b["kst"][g:g + 64, c, :], b["qst"][g:g + 64, c, :])
                            mm = fp32(bank(4 * d + 2 + h % 2, P, 256 + c * P), b["kst"][g:g + 64, c, :], b["kbT"][g:g + 64, c, :])
                        mm.then_inc(e["gram"].sem, 1)
                    for d in range(2):
                        b, e = dd[d], dv[d]
                        pe.wait_ge(e["bm"].sem, e["bm"].at(l, LEVELS * n + 1))
                        pe.wait_ge(e["diff"].sem, e["diff"].at(l, n + 1))
                        for h in range(4):
                            mm = fp32(h4(d, 0)[:, h, :], b["B0"][:, h, :], ident)
                        mm.then_inc(e["b1"].sem, 1)
                    for lv in range(1, LEVELS):
                        for d in range(2):
                            b, e = dd[d], dv[d]
                            pe.wait_ge(e["bm"].sem, e["bm"].at(l, LEVELS * n + lv + 1))
                            pe.wait_ge(e["tt"].sem, e["tt"].at(l, LEVELS * n + lv))
                            if lv == 1:
                                pe.wait_ge(e["lt"].sem, e["lt"].at(l, n + 1))
                            for h in range(4):
                                mm = fp32(h4(d, 1)[:, h, :], b["B0" if lv % 2 == 0 else "B1"][:, h, :], b["T"][:, h, :])
                            mm.then_inc(e["y"].sem, 1)
                        for d in range(2):
                            b, e = dd[d], dv[d]
                            pe.wait_ge(e["ye"].sem, e["ye"].at(l, (LEVELS - 1) * n + lv))
                            if lv < LEVELS - 1:
                                for h in range(4):
                                    mm = fp32(h4(d, 2)[:, h, :], b["TT"][:, h, :], b["Y"][:, h, :])
                                mm.then_inc(e["p1"].sem, 1)
                            for h in range(4):
                                mm = fp32(h4(d, 3)[:, h, :], b["Y"][:, h, :], b["TT"][:, h, :])
                            mm.then_inc(e["p2"].sem, 1)
                    for d in range(2):
                        b, e = dd[d], dv[d]
                        pe.wait_ge(e["kb"].sem, e["kb"].at(l, n + 1))
                        pe.wait_ge(e["tt"].sem, e["tt"].at(l, LEVELS * n + LEVELS))
                        for h in range(4):
                            g, c = 64 * (h % 2), h // 2
                            mm = fp32(h2(d, 0)[g:g + 64, c, :], b["kbg"][:, c, g:g + 64], b["TT"][:, h, :])
                        mm.then_inc(e["wt"].sem, 1)
                    for d in range(2):
                        b, e = dd[d], dv[d]
                        pe.wait_ge(e["wte"].sem, e["wte"].at(l, n + 1))
                        for c in range(2):
                            fp32(h2(d, 1)[:, c, :], b["nwT"][:, c, :], St[:, d, c, :])
                            for g in range(2):
                                mm = fp32(bank(4 * d + 1, 64, 128 * c + 64 * g), b["TT"][:, 2 * c + g, :], b["vb"][:, c, 64 * g:64 * g + 64],
                                          False, True, loose=True)
                        mm.then_inc(e["vn"].sem, 1)
                    for d in range(2):
                        b, e = dd[d], dv[d]
                        pe.wait_ge(e["vne"].sem, e["vne"].at(l, n + 1))
                        for c in range(2):
                            fp32(h2(d, 2)[:, c, :], St[:, d, c, :], b["qg"][:, c, :])
                            for g in range(2):
                                fp32(h2(d, 2)[64 * g:64 * g + 64, c, :], b["vnew"][:, c, 64 * g:64 * g + 64], b["AQ"][:, 2 * c + g, :],
                                     False, True, loose=True)
                        for c in range(2):
                            mm = fp32(h2(d, 3)[:, c, :], b["kdec"][:, c, :], b["vnew"][:, c, :])
                        mm.then_inc(e["os"].sem, 1)
                delta((0, 0), 0, Sctx)
                with pe.Fori(1, NT) as i:
                    delta((i, NT - i), i, Slat)
                for d in range(2):
                    pe.wait_ge(dv[d]["ose"].sem, dv[d]["ose"].at(l, NT))
                head_norm_rows(1, 2)
                head_norm_spread(1, 2)

                pe.wait_ge(oc_lo.sem, oc_lo.at(l, 1))
                for j in range(4):
                    s, use = (2, 0, 1, 2)[j], (3, 4, 4, 4)[j]
                    for c in range(2):
                        u, o = 2 * s + c, 2 * j + c
                        pe.wait_ge(split_full[u].sem, split_full[u].at(l, UN_MIX + (use - 1 if u == 3 else use) + 1))
                        pe.wait_ge(acc_used.sem, acc_used.at(l, ACC_OUT + o - 1))
                        chunk_product(2 + o % 2, u, k8, rhs=h_rhs).then_inc(unit_done[u].sem, 1)
                feed_forward(l, 1)

            pe.wait_ge(fin_sq, 1)
            for t in range(NT):
                for c in range(KC):
                    mm = fp32(bank(4, 1, t), sq8[:, c, t * P:(t + 1) * P], ones[:, 0:1], c == 0, c == KC - 1)
            mm.then_inc(fin_ss, 1)
            pe.wait_ge(fin_x, 1)
            n = 0
            for t in range(NT):
                for q in range(2):
                    if n >= 4:
                        pe.wait_ge(fin_e, n - 3)
                    for c in range(4):
                        mm = pe.transpose(bank(n % 4, 128, c * 128), xT[:, 4 * q + c, t * P:(t + 1) * P], ident)
                    mm.then_inc(fin_t, 1)
                    n += 1

        @block.scalar
        def _(act):
            def hi_part(l, s, c, use, un_use, kind, extra=0):
                u = 2 * s + c
                act.wait_ge(raw_full[s], raw_count(l, s, use, extra))
                act.wait_ge(unit_done[u].sem, unit_done[u].at(l, un_use))
                act.copy(un_view(un[u][0], kind), raw_view(s, c, kind)).then_inc(hi_done[u].sem, 1)

            def norm(l, st):
                act.wait_ge(x_ready.sem, x_ready.at(l, st + 1))
                for c in range(KC):
                    sq = act.activation(sq8[:, c, :], xT[:, c, :], ACT.Square)
                sq.then_inc(sq_ready.sem, 1)
                act.wait_ge(ms_ready.sem, ms_ready.at(l, st + 1))
                act.activation(nst[:, 5:10], nst[:, 0:5], ACT.Sqrt).then_inc(rt_ready.sem, 1)
                for c in range(KC):
                    act.wait_ge(t1_ready.sem, t1_ready.at(l, 8 * st + c + 1))
                    for s, lo, hi in STREAMS:
                        mm = act.activation(hh[:, c, lo:hi], t1[:, c % 2, lo:hi], ACT.Identity,
                                            bias=modT[:, 24 * st + c, s:s + 1])
                    mm.then_inc(hh_ready.sem, 1)

            def feed_forward(l, f):
                ub_ = [0] * 6 if f == 0 else [un_ff2(u) for u in range(6)]
                rb_ = RAW_FF1 if f == 0 else RAW_FF2

                def hi_w13(i, c):
                    for s in range(2):
                        hi_part(l, s, c, rb_ + i, ub_[2 * s + c] + i, "cols", f * OUT_BLOCKS[s])

                def hi_w2(i):
                    for g in range(2):
                        hi_part(l, 2, g, rb_ + i, ub_[4 + g] + i, "rows", f * OUT_BLOCKS[2])

                def chunk(i, c, more):
                    n = 2 * NB_FF * f + 2 * i + c
                    act.wait_ge(unit_done[c].sem, unit_done[c].at(l, ub_[c] + i + 1))
                    act.activation(sil[:, c, :], pair(0), ACT.Silu).then_inc(sil_ready.sem, 1)
                    act.wait_ge(gf_ready.sem, gf_ready.at(l, n + 1))
                    act.copy(gh[:, bass.ds(2 * (i % 2) + c, 1), :].rearrange("p o t -> p (o t)"), gf[:, c, :]).then_inc(gh_ready.sem, 1)
                    if more:
                        hi_w13(i + 1, c)
                for c in range(2):
                    hi_w13(0, c)
                norm(l, 0 if f == 0 else 2)
                for c in range(2):
                    chunk(0, c, True)
                with act.Fori(1, NB_FF - 1) as i:
                    hi_w2(i - 1)
                    for c in range(2):
                        chunk(i, c, True)
                hi_w2(NB_FF - 2)
                for c in range(2):
                    chunk(NB_FF - 1, c, False)
                hi_w2(NB_FF - 1)

            act.wait_ge(tables_in, 16)
            for n in range(0, 10, 2):
                act.wait_ge(xt_done, n + 1)
                t, q = n // 2, n % 2
                act.copy(xT[:, 4 * q:4 * q + 4, t * P:(t + 1) * P], bank(n % 4).rearrange("p (c t) -> p c t", c=4)).then_inc(xt_used, 1)
                act.wait_ge(xt_used, n + 2)
            act.wait_ge(cond_done, 1)
            act.activation(condE, bank(4, 16), ACT.Silu)
            act.activation(fcol, bank(4, 8, 16), ACT.Copy).then_inc(cond_exp, 1)

            with act.Fori(0, DEPTH) as l:
                feed_forward(l, 0)

                def hi_cols(s, use, un_use, cs=(0, 1), kind="cols", extra=0):
                    for c in cs:
                        hi_part(l, s, c, RAW_MIX + use, UN_MIX + un_use, kind, extra)

                def evac(q, c, s, use):
                    u = 2 * s + c
                    act.wait_ge(unit_done[u].sem, unit_done[u].at(l, UN_MIX + use + 1))
                    act.copy(PT[:, bass.ds(q, 1), :].rearrange("p o t -> p (o t)"), pair(2 + c)).then_inc(acc_used.sem, 1)
                hi_cols(0, 0, 0, kind="heads")
                norm(l, 1)
                with act.Fori(0, 3) as i:
                    for s in range(3):
                        hi_cols((s + 1) % 3, i + (s + 1) // 3, i + (s + 1) // 3)
                        for c in range(2):
                            evac(6 * i + (2 * s + c), c, s, i)
                hi_cols(1, 3, 3, (0,))
                for c in range(2):
                    evac(18 + c, c, 0, 3)
                act.wait_ge(unit_done[2].sem, unit_done[2].at(l, UN_MIX + 4))
                act.copy(PS[0:64, :], pair(2)[0:64, :]).then_inc(acc_used.sem, 1)
                act.drain().then_inc(acc_used.sem, 1)
                act.drain().then_inc(proj_done.sem, 1)

                for n in range(6):
                    act.wait_ge(cv_ready.sem, cv_ready.at(l, n + 1))
                    act.activation(PT[:, C_QC + n, :], cv[:, n % 2, :], ACT.Silu).then_inc(cv_used.sem, 1)
                act.activation(PT[:, C_ZC:C_ZC + 2, :], PT[:, C_ZC:C_ZC + 2, :], ACT.Silu)
                act.drain()
                for n, c in enumerate(NORMS):
                    sq = act.activation(sq7[:, n, :], PT[:, c, :], ACT.Square)
                sq.then_inc(sq7_ready.sem, 1)
                act.wait_ge(ob_ready.sem, ob_ready.at(l, 1))
                act.copy(hh[:, 2:4, :], PT[:, C_GB:C_GB + 2, :]).then_inc(ob_hi.sem, 1)
                act.wait_ge(nr_done.sem, nr_done.at(l, 1))
                act.activation(rrow[0:14, 1, :], pair(0)[0:14, :], ACT.Sqrt, bias=tb[0:14, T_SC + 1:T_SC + 2],
                               scale=tb[0:14, T_SC:T_SC + 1]).then_inc(nq_ready.sem, 1)

                act.wait_ge(tr_done.sem, tr_done.at(l, 1))
                act.copy(vtok[:, 1:5, :], bank(0).rearrange("p (t n) -> p t n", t=4))
                act.copy(vtok[:, 5, :], bank(1, 128))
                act.copy(kct, bank(1, 128, 128))
                act.copy(kall[:, 0:P], bank(1, 128, 256)).then_inc(tr_used.sem, 1)

                def attend(n, latent):
                    w = T if latent else P

                    def exps(k):
                        act.wait_ge(nmax_ready.sem, nmax_ready.at(l, 4 * n + k + 1))
                        j = 4 * (k % 2)
                        act.activation(pexp[:, k % 2, 0:w], pair(k % 2)[:, 0:w], ACT.Exp, bias=ast[:, j + 1:j + 2],
                                       scale=HEAD ** -0.5, accum_out=ast[:, j + 2:j + 3]).then_inc(p_exp.sem, 1)

                    def out(k):
                        act.wait_ge(pT_done.sem, pT_done.at(l, 4 * n + k + 1))
                        if latent:
                            act.copy(pTs, tiles5(4)).then_inc(pT_used.sem, 1)
                        else:
                            act.copy(pTs[:, 0, :], tiles5(4)[:, 0, :]).then_inc(pT_used.sem, 1)
                    exps(0)
                    exps(1)
                    for k in range(4):
                        if k or latent:
                            act.wait_ge(pv_done.sem, pv_done.at(l, 4 * n + k))
                        out(k)
                        if k + 2 < 4:
                            exps(k + 2)
                attend(0, False)
                with act.Fori(1, NT) as i:
                    attend(i, True)

                for c in range(2):
                    act.wait_ge(f1_done.sem, f1_done.at(l, c + 1))
                    if c:
                        act.wait_ge(f2_done.sem, f2_done.at(l, c))
                    act.copy(xcs, ps_all[:, 0:1280].rearrange("p (t n) -> p t n", t=5)).then_inc(f1_used.sem, 1)
                    act.wait_ge(f2_done.sem, f2_done.at(l, c + 1))
                    act.copy(hh[:, 6 + c, :].rearrange("p (t n) -> p t n", t=5), tiles5(4)).then_inc(f_hi.sem, 1)

                act.activation(er, PS[0:8, :], ACT.Exp, scale=-1.0)
                act.activation(adt[32:40, 2:3], adt[32:40, 0:1], ACT.Exp).then_inc(e_rows.sem, 1)
                act.wait_ge(sp_x.sem, sp_x.at(l, 1))
                act.activation(PT[32:40, 9, :], PS[32:40, :], ACT.Abs)
                act.drain()
                act.activation(PT[32:40, 9, :], PT[32:40, 9, :], ACT.Exp, scale=-1.0)
                act.drain()
                act.activation(PT[32:40, 9, :], PT[32:40, 9, :], ACT.Ln, bias=ones[32:40, 0:1]).then_inc(e_ln.sem, 1)
                for k in range(4):
                    act.wait_ge(kv_done.sem, kv_done.at(l, k + 1))
                    act.copy((ktok, vtokc)[k // 2][:, k % 2], tiles5((4, 6)[k % 2])).then_inc(kv_used.sem, 1)
                act.wait_ge(gc_ready.sem, gc_ready.at(l, 1))
                act.activation(gk(G_EG), gk(G_GC), ACT.Exp)
                act.activation(gk(G_KD), gk(G_T), ACT.Exp)
                act.activation(gk(G_EGL), bank(1, 40, 40).rearrange("p (t e) -> p t e", t=NT), ACT.Exp).then_inc(gexp_ready.sem, 1)
                act.wait_ge(gr_done.sem, gr_done.at(l, 1))
                act.copy(gcr.rearrange("p (t n) -> p t n", t=5), tiles5(2)[0:8])
                act.activation(er.rearrange("p (t n) -> p t n", t=5), tiles5(2)[0:8], ACT.Exp).then_inc(gr_used.sem, 1)

                def delta(n):
                    for d in range(2):
                        b, e = dd[d], dv[d]
                        act.wait_ge(e["diff"].sem, e["diff"].at(l, n + 1))
                        act.activation(b["E"], b["E"], ACT.Exp).then_inc(e["decay"].sem, 1)
                    for lv in range(1, LEVELS):
                        for d in range(2):
                            b, e = dd[d], dv[d]
                            act.wait_ge(e["y"].sem, e["y"].at(l, (LEVELS - 1) * n + lv))
                            act.copy(b["Y"], bank(4 * d + 1).rearrange("p (h t) -> p h t", h=4)).then_inc(e["ye"].sem, 1)
                    for d in range(2):
                        b, e = dd[d], dv[d]
                        act.wait_ge(e["wt"].sem, e["wt"].at(l, n + 1))
                        act.mul(b["nwT"], bank(4 * d, 256).rearrange("p (c t) -> p c t", c=2), -1.0).then_inc(e["wte"].sem, 1)
                    for d in range(2):
                        b, e = dd[d], dv[d]
                        act.wait_ge(e["vn"].sem, e["vn"].at(l, n + 1))
                        act.copy(b["vnew"], bank(4 * d + 1, 256).rearrange("p (c t) -> p c t", c=2)).then_inc(e["vne"].sem, 1)
                delta(0)
                with act.Fori(1, NT) as i:
                    delta(i)
                act.wait_ge(oc_ready.sem, oc_ready.at(l, 1))
                act.activation(PT[:, 4:6, :], oC, ACT.Square).then_inc(sq7_ready.sem, 1)
                act.wait_ge(nr_done.sem, nr_done.at(l, 2))
                act.activation(PT[0:14, 9, :], pair(0)[0:14, :], ACT.Sqrt, bias=tb[0:14, T_SC + 1:T_SC + 2],
                               scale=1.0 / HEAD).then_inc(nq_ready.sem, 1)
                act.wait_ge(oc_gate.sem, oc_gate.at(l, 1))
                act.copy(hh[:, 4:6, :], oC).then_inc(oc_hi.sem, 1)

                for j in range(4):
                    s, use = (2, 0, 1, 2)[j], (3, 4, 4, 4)[j]
                    for c in range(2):
                        hi_cols(s, use, use - 1 if 2 * s + c == 3 else use, (c,), extra=j // 3 + 1)
                act.wait_ge(st_out.sem, st_out.at(l, 64))
                feed_forward(l, 1)

            act.wait_ge(x_ready.sem, 3 * DEPTH + 1)
            for c in range(KC):
                sq = act.activation(sq8[:, c, :], xT[:, c, :], ACT.Square)
            sq.then_inc(fin_sq, 1)
            act.wait_ge(fin_ms, 1)
            act.activation(nst[:, 5:10], nst[:, 0:5], ACT.Sqrt).then_inc(fin_rt, 1)

        @block.vector
        def _(ve):
            def lo_part(l, s, c, un_use, kind, frees):
                u = 2 * s + c
                ve.wait_ge(hi_done[u].sem, hi_done[u].at(l, un_use + 1))
                ve.tensor_tensor(un_view(un[u][1], kind), raw_view(s, c, kind), un_view(un[u][0], kind).bitcast(F32),
                                 ALU.subtract).then_inc(split_full[u].sem, 1)
                if frees:
                    ve.drain().then_inc(raw_free[s].sem, 1)

            def norm(l, st):
                ve.wait_ge(ss_done.sem, ss_done.at(l, st + 1))
                ve.tensor_scalar(nst[:, 0:5], bank(4, 5), 1.0 / D, EPS, ALU.mult, ALU.add).then_inc(ms_ready.sem, 1)
                ve.wait_ge(rt_ready.sem, rt_ready.at(l, st + 1))
                ve.reciprocal(nst[:, 10:15], nst[:, 5:10])
                ve.drain()
                for t in range(NT):
                    dg = ve.tensor_scalar(diag[:, t, :], ident, nst[:, 10 + t:11 + t], None, ALU.mult)
                dg.then_inc(diag_ready.sem, 1)
                ve.wait_ge(rb_done.sem, rb_done.at(l, st + 1))
                rb = ps_all[:, 5 * 512 + 384:7 * 512]

                def scaled(c):
                    for s, lo, hi in STREAMS:
                        i = ve.scalar_tensor_tensor(t1[:, c % 2, lo:hi], xT[:, c, lo:hi], mA[:, st, c, s:s + 1], rb[:, lo:hi],
                                                    ALU.mult, ALU.mult)
                    i.then_inc(t1_ready.sem, 1)
                scaled(0)
                scaled(1)
                for c in range(KC):
                    ve.wait_ge(hh_ready.sem, hh_ready.at(l, 8 * st + c + 1))
                    for s, lo, hi in STREAMS:
                        i = ve.scalar_tensor_tensor(hl[:, c, lo:hi], t1[:, c % 2, lo:hi], modT[:, 24 * st + c, s:s + 1],
                                                    hh[:, c, lo:hi].bitcast(F32), ALU.add, ALU.subtract)
                    i.then_inc(h_ready.sem, 1)
                    if c + 2 < KC:
                        ve.drain()
                        scaled(c + 2)

            def residual(o, q, gate_chunk):
                for s, lo, hi in STREAMS:
                    i = ve.scalar_tensor_tensor(xT[:, o, lo:hi], pair(q)[:, lo:hi], modT[:, gate_chunk + o, s:s + 1],
                                                xT[:, o, lo:hi], ALU.mult, ALU.add)
                i.then_inc(acc_used.sem, 1)

            def feed_forward(l, f):
                ub_ = [0] * 6 if f == 0 else [un_ff2(u) for u in range(6)]
                st = 0 if f == 0 else 2

                def lo_w13(i, c):
                    for s in range(2):
                        lo_part(l, s, c, ub_[2 * s + c] + i, "cols", c == 1)

                def lo_w2(i):
                    for g in range(2):
                        lo_part(l, 2, g, ub_[4 + g] + i, "rows", g == 1)

                def chunk(i, c, more):
                    n = 2 * NB_FF * f + 2 * i + c
                    ve.wait_ge(sil_ready.sem, sil_ready.at(l, n + 1))
                    ve.wait_ge(unit_done[2 + c].sem, unit_done[2 + c].at(l, ub_[2 + c] + i + 1))
                    ve.tensor_tensor(gf[:, c, :], pair(1), sil[:, c, :], ALU.mult).then_inc(gf_ready.sem, 1)
                    ve.wait_ge(gh_ready.sem, gh_ready.at(l, n + 1))
                    g = bass.ds(2 * (i % 2) + c, 1)
                    ve.tensor_tensor(gl[:, g, :].rearrange("p o t -> p (o t)"), gf[:, c, :],
                                     gh[:, g, :].rearrange("p o t -> p (o t)").bitcast(F32), ALU.subtract).then_inc(g_ready.sem, 1)
                    if more:
                        lo_w13(i + 1, c)

                def down(i):
                    for o in range(KC):
                        if o < KC - 1:
                            ve.wait_ge(y_done.sem, y_done.at(l, 7 * NB_FF * f + 7 * i + o + 1))
                        else:
                            ve.wait_ge(unit_done[5].sem, unit_done[5].at(l, ub_[5] + i + 1))
                        residual(o, 2 + o % 2, 24 * st + 16)
                for c in range(2):
                    lo_w13(0, c)
                norm(l, st)
                for c in range(2):
                    chunk(0, c, True)
                with ve.Fori(1, NB_FF - 1) as i:
                    lo_w2(i - 1)
                    for c in range(2):
                        chunk(i, c, True)
                    down(i - 1)
                lo_w2(NB_FF - 2)
                for c in range(2):
                    chunk(NB_FF - 1, c, False)
                down(NB_FF - 2)
                lo_w2(NB_FF - 1)
                down(NB_FF - 1)
                ve.drain().then_inc(x_ready.sem, 1)

            for s in range(2):
                ve.sem_inc(acc_used.sem, 1)
            ve.wait_ge(tables_in, 16)
            for n in range(1, 10, 2):
                ve.wait_ge(xt_done, n + 1)
                t, q = n // 2, n % 2
                ve.wait_ge(xt_used, n)
                ve.tensor_copy(xT[:, 4 * q:4 * q + 4, t * P:(t + 1) * P], bank(n % 4).rearrange("p (c t) -> p c t", c=4)).then_inc(xt_used, 1)
            ve.wait_ge(cond_exp, 1)
            ve.tensor_copy(condT, condE.rearrange("p (s k) -> p k s", s=2)).then_inc(cond_ready, 1)
            ve.drain().then_inc(x_ready.sem, 1)

            with ve.Fori(0, DEPTH) as l:
                ve.wait_ge(vecT_done.sem, vecT_done.at(l, 1))
                ve.tensor_copy(vcol, bank(6, 128))
                ve.drain().then_inc(cond_ready, 1)
                ve.wait_ge(raw_free[2].sem, raw_free[2].at(l, NB_MOD // 3))
                ve.tensor_tensor(modT, bank(7, 2 * MODC).rearrange("p (c s) -> p c s", s=2),
                                 vcol[:, V_MODB:V_MODB + MODC].rearrange("p (c o) -> p c o", o=1).to_broadcast([P, MODC, 2]), ALU.add)
                ve.drain()
                for st in range(3):
                    gain = vcol[:, V_NORM + 8 * st:V_NORM + 8 * st + 8].rearrange("p (c o) -> p c o", o=1).to_broadcast([P, KC, 2])
                    ve.scalar_tensor_tensor(mA[:, st], modT[:, 24 * st + 8:24 * st + 16, :], 1.0, gain, ALU.add, ALU.mult)
                    if st != 1:
                        g = modT[:, 24 * st + 16:24 * st + 24, :]
                        ve.tensor_scalar(g, g, 0.5, None, ALU.mult)
                ve.drain()
                feed_forward(l, 0)

                def lo_cols(s, un_use, cs=(0, 1), kind="cols"):
                    for c in cs:
                        lo_part(l, s, c, UN_MIX + un_use, kind, c == cs[-1])
                lo_cols(0, 0, kind="heads")
                norm(l, 1)
                with ve.Fori(0, 3) as i:
                    for s in range(3):
                        lo_cols((s + 1) % 3, i + (s + 1) // 3)
                lo_cols(1, 3, (0,))

                ve.wait_ge(proj_done.sem, proj_done.at(l, 1))

                def conv(dst, src, w):
                    ve.tensor_scalar(dst, src, vcol[:, w(1):w(1) + 1], None, ALU.mult)
                    ve.drain()
                    for _, lo, hi in STREAMS:
                        ve.scalar_tensor_tensor(dst[:, lo + 1:hi], src[:, lo:hi - 1], vcol[:, w(0):w(0) + 1], dst[:, lo + 1:hi], ALU.mult, ALU.add)
                    ve.drain()
                    for _, lo, hi in STREAMS:
                        i = ve.scalar_tensor_tensor(dst[:, lo:hi - 1], src[:, lo + 1:hi], vcol[:, w(2):w(2) + 1], dst[:, lo:hi - 1], ALU.mult, ALU.add)
                    return i
                for n in range(6):
                    if n >= 2:
                        ve.wait_ge(cv_used.sem, cv_used.at(l, n - 1))
                    conv(cv[:, n % 2, :], PT[:, C_QC + n, :], lambda j, n=n: V_CONVC + 6 * j + n).then_inc(cv_ready.sem, 1)
                for c in range(2):
                    ve.tensor_tensor(PT[:, C_XB + c, :], PT[:, C_XB + c, :], PT[:, C_GC + c, :], ALU.mult)
                    ve.drain()
                    conv(PT[:, C_GC + c, :], PT[:, C_XB + c, :], lambda j, c=c: V_CONVB + 2 * j + c)
                    ve.drain()
                    i = ve.tensor_tensor(PT[:, C_GB + c, :], PT[:, C_GB + c, :], PT[:, C_GC + c, :], ALU.mult)
                i.then_inc(ob_ready.sem, 1)
                ve.wait_ge(ob_hi.sem, ob_hi.at(l, 1))
                ve.tensor_tensor(hl[:, 2:4, :], PT[:, C_GB:C_GB + 2, :], hh[:, 2:4, :].bitcast(F32), ALU.subtract)

                ve.wait_ge(nq_ready.sem, nq_ready.at(l, 1))
                ve.reciprocal(rrow[0:14, 0, :], rrow[0:14, 1, :]).then_inc(nrow_ready.sem, 1)
                for n, c in enumerate(NORMS):
                    ve.wait_ge(bc_done.sem, bc_done.at(l, n + 1))
                    if n < 3:
                        v = V_QN if n < 2 else V_KN
                        i = ve.scalar_tensor_tensor(PT[:, c, :], PT[:, c, :], vcol[:, v:v + 1], pair(1 + n % 2), ALU.mult, ALU.mult)
                    else:
                        i = ve.tensor_tensor(PT[:, c, :], PT[:, c, :], pair(1 + n % 2), ALU.mult)
                    i.then_inc(bc_used.sem, 1)

                ve.wait_ge(mt_in.sem, mt_in.at(l, 80))
                for n, c in enumerate((C_QA, C_QA + 1, C_KA)):
                    ve.wait_ge(rot_done.sem, rot_done.at(l, n + 1))
                    ve.tensor_tensor(rtmp, bank(2 + n), ub[:, U_SIN:U_SIN + 512], ALU.mult)
                    ve.tensor_tensor(PT[:, c, CTX:T], PT[:, c, CTX:T], ub[:, U_COS:U_COS + 512], ALU.mult)
                    ve.drain()
                    i = ve.tensor_tensor(kall[:, CTX:T] if c == C_KA else PT[:, c, CTX:T], PT[:, c, CTX:T], rtmp, ALU.add)
                    ve.drain()
                ve.drain().then_inc(roped.sem, 1)

                def attend(n, t, latent):
                    w = T if latent else P
                    ve.tensor_copy(qs, PT[:, C_QA:C_QA + 2, bass.ds(t * P, P)]).then_inc(qs_ready.sem, 1)

                    def peak(k):
                        j = 4 * (k % 2)
                        ve.wait_ge(s_done.sem, s_done.at(l, 4 * n + k + 1))
                        ve.tensor_reduce(ast[:, j:j + 1], pair(k % 2)[:, 0:w], AX.X, ALU.max)
                        ve.drain()
                        ve.tensor_scalar(ast[:, j + 1:j + 2], ast[:, j:j + 1], -HEAD ** -0.5, None, ALU.mult).then_inc(nmax_ready.sem, 1)

                    def scale(k):
                        j = 4 * (k % 2)
                        ve.wait_ge(p_exp.sem, p_exp.at(l, 4 * n + k + 1))
                        ve.reciprocal(ast[:, j + 3:j + 4], ast[:, j + 2:j + 3])
                        ve.drain()
                        ve.tensor_scalar(pexp[:, k % 2, 0:w], pexp[:, k % 2, 0:w], ast[:, j + 3:j + 4], None, ALU.mult).then_inc(p_ready.sem, 1)

                    def heads_out(c):
                        ve.wait_ge(pv_done.sem, pv_done.at(l, 4 * n + 2 * c + 2))
                        o = bank(6 + c, 128)
                        hs = hh[:, c, bass.ds(t * P, P)]
                        ve.tensor_copy(hs, o)
                        ve.drain()
                        ve.tensor_tensor(hl[:, c, bass.ds(t * P, P)], o, hs.bitcast(F32), ALU.subtract).then_inc(pv_used.sem, 1)
                    peak(0)
                    peak(1)
                    for k in range(4):
                        scale(k)
                        if k + 2 < 4:
                            peak(k + 2)
                        if k == 2:
                            heads_out(0)
                    heads_out(1)
                attend(0, 0, False)
                with ve.Fori(1, NT) as i:
                    attend(i, i, True)

                for c in range(2):
                    ve.wait_ge(f_hi.sem, f_hi.at(l, c + 1))
                    ve.tensor_tensor(hl[:, 6 + c, :].rearrange("p (t n) -> p t n", t=5), tiles5(4),
                                     hh[:, 6 + c, :].rearrange("p (t n) -> p t n", t=5).bitcast(F32), ALU.subtract).then_inc(f_lo.sem, 1)

                ve.tensor_scalar(PS[32:40, :], PS[32:40, :], adt[32:40, 1:2], None, ALU.add).then_inc(sp_x.sem, 1)
                ve.wait_ge(e_rows.sem, e_rows.at(l, 1))
                ve.tensor_scalar(er, er, 1.0, None, ALU.add)
                ve.drain()
                ve.reciprocal(PS[0:8, :], er)
                ve.wait_ge(e_ln.sem, e_ln.at(l, 1))
                ve.scalar_tensor_tensor(PS[32:40, :], PS[32:40, :], 0.0, PT[32:40, 9, :], ALU.max, ALU.add)
                ve.drain()
                ve.tensor_scalar(PS[32:40, :], PS[32:40, :], adt[32:40, 2:3], -1.0, ALU.mult, ALU.mult).then_inc(rows_ready.sem, 1)
                ve.wait_ge(gt_done.sem, gt_done.at(l, 1))
                ve.tensor_copy(gsm[:, 0:40], bank(0, 40))
                ve.tensor_copy(gsm[:, 40:80], bank(2, 40)).then_inc(gt_used.sem, 1)
                ve.wait_ge(gc_done.sem, gc_done.at(l, 1))
                ve.tensor_copy(gk(G_GC), bank(1, 40).rearrange("p (t e) -> p t e", t=NT))
                ve.drain()
                ve.tensor_tensor(gk(G_T), bank(1, 40, 40).rearrange("p (t e) -> p t e", t=NT), gk(G_GC), ALU.subtract)
                ve.drain()
                ve.tensor_scalar(gk(G_T), gk(G_T), 0.0, None, ALU.min).then_inc(gc_ready.sem, 1)
                ve.wait_ge(gexp_ready.sem, gexp_ready.at(l, 1))
                ve.tensor_tensor(gk(G_BG), gk(G_BETA), gk(G_EG), ALU.mult)
                ve.drain().then_inc(gcol_ready.sem, 1)
                ve.wait_ge(kv_used.sem, kv_used.at(l, 4))
                ve.wait_ge(gr_used.sem, gr_used.at(l, 1))
                ve.wait_ge(oz_ready.sem, oz_ready.at(l, 1))

                def delta(tiles, n, St):
                    cols = [bass.ds(t * P, P) for t in tiles]
                    ds1 = [bass.ds(t, 1) for t in tiles]
                    b4 = lambda d, k: bank(4 * d + k).rearrange("p (h t) -> p h t", h=4)
                    id4 = ident.rearrange("p (o n) -> p o n", o=1).to_broadcast([P, 4, P])

                    def col(k, d, h, p0=0, p1=P):
                        c = gsm[p0:p1, 40 * k:40 * k + 40].rearrange("p (t e) -> p t e", t=NT)
                        return c[:, ds1[d], 4 * d + h:4 * d + h + 1].rearrange("p o e -> p (o e)")
                    for d in range(2):
                        b, e = dd[d], dv[d]
                        ve.wait_ge(e["bcast"].sem, e["bcast"].at(l, n + 1))
                        settle(ve)
                        for h in range(4):
                            i = ve.scalar_tensor_tensor(b["E"][:, h, :], b4(d, 0)[:, h, :], col(G_GC, d, h), negm(d), ALU.subtract, ALU.min)
                        i.then_inc(e["diff"].sem, 1)
                        bb = bank(4 * d + 1).rearrange("p (k c t) -> p k c t", k=2, c=2)
                        ve.tensor_copy(b["kst"], PT[:, C_KC:C_KC + 2, cols[d]])
                        ve.tensor_copy(b["qst"], PT[:, C_QC:C_QC + 2, cols[d]])
                        ve.tensor_tensor(b["qg"], bb[:, 0], PT[:, C_QC:C_QC + 2, cols[d]], ALU.mult)
                        ve.tensor_tensor(b["kbT"], bb[:, 1], PT[:, C_KC:C_KC + 2, cols[d]], ALU.mult).then_inc(e["staged"].sem, 1)
                    for d in range(2):
                        b, e = dd[d], dv[d]
                        ve.wait_ge(e["decay"].sem, e["decay"].at(l, n + 1))
                        ve.wait_ge(e["gram"].sem, e["gram"].at(l, n + 1))
                        gram = ps_all[:, (4 * d + 2) * 512:(4 * d + 4) * 512].rearrange("p (g k c t) -> p k c g t", g=2, k=2, c=2)
                        cg = lambda x: x.rearrange("p (c g) t -> p c g t", c=2)
                        ve.tensor_tensor(cg(b["LT"]), gram[:, 1], cg(b["E"]), ALU.mult).then_inc(e["lt"].sem, 1)
                        ve.tensor_tensor(cg(b["AQ"]), gram[:, 0], cg(b["E"]), ALU.mult)
                    for d in range(2):
                        b, e = dd[d], dv[d]
                        ve.wait_ge(e["b1"].sem, e["b1"].at(l, n + 1))
                        ve.tensor_tensor(b["T"], id4, b4(d, 0), ALU.subtract)
                        ve.tensor_tensor(b["TT"], id4, b["B0"], ALU.subtract).then_inc(e["tt"].sem, 1)
                        for src, k, dst in ((ktok, G_BG, "kbg"), (vtokc, G_BETA, "vb"), (ktok, G_KD, "kdec")):
                            g = gk(k)[:, ds1[d], 4 * d:4 * d + 4].rearrange("p o h -> p (o h)").rearrange("p (c g u) -> p c g u", c=2, g=2)
                            i = ve.tensor_tensor(b[dst].rearrange("p c (g n) -> p c g n", g=2),
                                                 src[:, :, ds1[d], :].rearrange("p c o n -> p c (o n)").rearrange("p c (g n) -> p c g n", g=2),
                                                 g.to_broadcast([P, 2, 2, HEAD]), ALU.mult)
                        i.then_inc(e["kb"].sem, 1)
                    for lv in range(1, LEVELS):
                        for d in range(2):
                            b, e = dd[d], dv[d]
                            if lv < LEVELS - 1:
                                ve.wait_ge(e["p1"].sem, e["p1"].at(l, (LEVELS - 2) * n + lv))
                                ve.tensor_tensor(b["T"], b["T"], b4(d, 2), ALU.subtract)
                            ve.wait_ge(e["p2"].sem, e["p2"].at(l, (LEVELS - 1) * n + lv))
                            ve.tensor_tensor(b["TT"], b["TT"], b4(d, 3), ALU.subtract).then_inc(e["tt"].sem, 1)
                    for d in range(2):
                        b, e = dd[d], dv[d]
                        ve.wait_ge(e["os"].sem, e["os"].at(l, n + 1))
                        ve.tensor_tensor(oC[:, :, cols[d]], oC[:, :, cols[d]], bank(4 * d + 2, 256).rearrange("p (c t) -> p c t", c=2), ALU.add)
                        for c in range(2):
                            for g in range(2):
                                r = slice(64 * g, 64 * g + 64)
                                sv = St[r, d, c, r]
                                i = ve.scalar_tensor_tensor(sv, sv, col(G_EGL, d, 2 * c + g, 64 * g, 64 * g + 64),
                                                            ps_all[r, (4 * d + 3) * 512 + 128 * c + 64 * g:(4 * d + 3) * 512 + 128 * c + 64 * g + 64],
                                                            ALU.mult, ALU.add)
                        i.then_inc(e["ose"].sem, 1)
                        ve.drain()
                delta((0, 0), 0, Sctx)
                ve.wait_ge(st_in, 48 + 64 * (l + 1))
                settle(ve)
                with ve.Fori(1, NT) as i:
                    delta((i, NT - i), i, Slat)
                ve.drain().then_inc(oc_ready.sem, 1)

                ve.wait_ge(nq_ready.sem, nq_ready.at(l, 2))
                ve.reciprocal(PT[0:14, 8, :], PT[0:14, 9, :]).then_inc(nrow_ready.sem, 1)
                for c in range(2):
                    ve.wait_ge(bc_done.sem, bc_done.at(l, 8 + c))
                    ve.scalar_tensor_tensor(oC[:, c, :], oC[:, c, :], vcol[:, V_DN:V_DN + 1], pair(1 + c % 2), ALU.mult, ALU.mult).then_inc(bc_used.sem, 1)
                ve.drain()
                ve.tensor_tensor(oC, oC, PT[:, C_ZC:C_ZC + 2, :], ALU.mult).then_inc(oc_gate.sem, 1)
                ve.wait_ge(oc_hi.sem, oc_hi.at(l, 1))
                ve.tensor_tensor(hl[:, 4:6, :], oC, hh[:, 4:6, :].bitcast(F32), ALU.subtract).then_inc(oc_lo.sem, 1)

                for j in range(4):
                    s, use = (2, 0, 1, 2)[j], (3, 4, 4, 4)[j]
                    for c in range(2):
                        lo_part(l, s, c, UN_MIX + (use - 1 if 2 * s + c == 3 else use), "cols", c == 1)
                    if j:
                        out_residual(ve, l, j - 1, residual, unit_done)
                ve.wait_ge(st_out.sem, st_out.at(l, 64))
                out_residual(ve, l, 3, residual, unit_done)
                ve.drain().then_inc(x_ready.sem, 1)
                feed_forward(l, 1)

            ve.wait_ge(fin_ss, 1)
            ve.tensor_scalar(nst[:, 0:5], bank(4, 5), 1.0 / D, EPS, ALU.mult, ALU.add).then_inc(fin_ms, 1)
            ve.wait_ge(fin_rt, 1)
            ve.reciprocal(nst[:, 10:15], nst[:, 5:10])
            for c in range(KC):
                i = ve.tensor_scalar(xT[:, c, :], xT[:, c, :], fcol[:, c:c + 1], None, ALU.mult)
            i.then_inc(fin_x, 1)
            n = 0
            for t in range(NT):
                for q in range(2):
                    ve.wait_ge(fin_t, n + 1)
                    ve.tensor_scalar(fin_row[:, t, 512 * q:512 * q + 512], bank(n % 4), nst[:, 10 + t:11 + t], None, ALU.mult).then_inc(fin_e, 1)
                    n += 1


def out_residual(ve, l, j, residual, unit_done):
    s, use = (2, 0, 1, 2)[j], (3, 4, 4, 4)[j]
    for c in range(2):
        u = 2 * s + c
        ve.wait_ge(unit_done[u].sem, unit_done[u].at(l, UN_MIX + (use - 1 if u == 3 else use) + 1))
        residual(2 * j + c, 2 + c, 24 + 16)


def _tables():
    import numpy as np
    p = np.arange(P)
    tb = np.zeros((P, T_ALL))
    tb[:, T_ID:T_ID + P] = np.eye(P)
    tb[:, T_ONE:T_ONE + P] = 1
    j, i = p[:, None], p[None, :]
    for lv in range(LEVELS):
        n = 2 ** lv
        m = ((i // (2 * n)) == (j // (2 * n))) & (j // n % 2 == 0) & (i // n % 2 == 1)
        tb[:, T_MASK + lv * P:T_MASK + (lv + 1) * P] = m
        tb[:, T_MASK + (LEVELS + lv) * P:T_MASK + (LEVELS + lv + 1) * P] = m.T
    tb[:, T_NEG:T_NEG + P] = np.where(i >= j, 0, -1e30)
    tb[:, T_NEG + P:T_NEG + 2 * P] = np.where(i <= j, 0, -1e30)
    tb[:, T_TRI:T_TRI + P] = j <= i
    tb[:, T_TRI + P:T_TRI + 2 * P] = j >= i
    for c in range(7):
        for g in range(2):
            r = 2 * c + g
            tb[64 * g:64 * g + 64, T_SUM + 14 * c + r] = 1
            tb[r, T_BC + 128 * c + 64 * g:T_BC + 128 * c + 64 * g + 64] = HEAD ** -0.5 if c >= 5 else 1
            tb[r, T_SC] = 1.0 / HEAD if c < 3 else 1
    tb[:, T_SC + 1] = EPS
    q = HEAD // 4
    rot = np.zeros((P, P))
    for m in range(P):
        if m % (2 * q) < q:
            rot[m + q, m] = -1
        else:
            rot[m - q, m] = 1
    tb[:, T_ROT:T_ROT + P] = rot
    ub = np.zeros((P, U_ALL))
    inv = (np.float32(10000.0) ** (-np.arange(q, dtype=np.float32) / np.float32(q))).astype(np.float32)
    tok = np.arange(LAT)
    for m in range(P):
        f = m % HEAD
        pos = (tok // 64 if f < HEAD // 2 else tok % 64).astype(np.float32)
        ang = (pos * inv[f % q]).astype(np.float32).astype(np.float64)
        ub[m, U_COS:U_COS + LAT] = np.cos(ang)
        ub[m, U_SIN:U_SIN + LAT] = np.sin(ang)
    f = np.arange(HEAD)
    w = 2 * np.pi * (f[:, None] * f[None, :] % HEAD) / HEAD
    for g in range(2):
        r = slice(64 * g, 64 * g + 64)
        ub[r, U_DFT + 64 * g:U_DFT + 64 * g + 64] = np.cos(w)
        ub[r, U_DFT + P + 64 * g:U_DFT + P + 64 * g + 64] = np.sin(w)
    for n, uc, us in ((LAT, U_CL, U_SL), (CTX, U_CC, U_SCX)):
        k = np.arange(n)
        w = 2 * np.pi * (k[:, None] * k[None, :] % n) / n
        s = 1 / np.sqrt(n * HEAD)
        for t in range(n // P):
            ub[:, uc + t * n:uc + (t + 1) * n] = np.cos(w[t * P:(t + 1) * P]) * s
            ub[:, us + t * n:us + (t + 1) * n] = -np.sin(w[t * P:(t + 1) * P]) * s
    return tb.astype(np.float32), ub.astype(np.float32)


_INS = ["x_prompt", "x_sample", "c", "cache_k", "cache_v", "state_delta", "c_ctx", "mod_w", "mod_b", "norm_ffn1", "norm_mix",
        "norm_ffn2", "ffn1_w1", "ffn1_w3", "ffn1_w2", "ffn2_w1", "ffn2_w3", "ffn2_w2", "w_in", "w_out", "q_norm", "k_norm",
        "conv_b_w", "conv_c_w", "delta_a_log", "delta_dt_bias", "delta_norm", "final_norm"]
_OUTS = [(1, CTX, D), (1, LAT, D), (1, DEPTH, 2, CTX, HEAD), (1, DEPTH, 2, CTX, HEAD), (1, DEPTH, 2, 4, HEAD, HEAD)]


def kernel(**inputs):
    import numpy as np
    import concourse.bacc as bacc
    from concourse.bass_utils import run_bass_kernel_spmd

    nc = bacc.Bacc("TRN2", target_bir_lowering=False, num_devices=1)
    arrays, args = {}, {}
    for name in _INS:
        arrays[name] = np.ascontiguousarray(inputs[name])
        args[name] = nc.dram_tensor(name, arrays[name].shape, F32, kind="ExternalInput").ap()
    extra = []
    for name, value in zip(("tables", "mixer_tables"), _tables()):
        arrays[name] = value
        extra.append(nc.dram_tensor(name, value.shape, F32, kind="ExternalInput").ap())
    outs = [nc.dram_tensor(f"out{i}", shape, F32, kind="ExternalOutput").ap() for i, shape in enumerate(_OUTS)]
    build(nc, args, *extra, outs)
    r = run_bass_kernel_spmd(nc, [arrays], core_ids=[0])
    return tuple(r.results[0][f"out{i}"] for i in range(len(_OUTS)))
```

```python
from contextlib import ExitStack

import concourse.bass as bass
from concourse import mybir

F32 = mybir.dt.float32
F32R = mybir.dt.float32r
ALU = mybir.AluOpType
ACT = mybir.ActivationFunctionType
AX = mybir.AxisListType

P = 128
D = 1024
KC = D // P
DEPTH = 2
CTX, LAT = 128, 512
T = CTX + LAT
NT = T // P
FF = 2816
HEAD = 64
PROJ = 2576
NMOD = 9
MODC = NMOD * KC
EPS = 1e-6
BLK = 256
NB_FF = FF // BLK
NB_MOD = NMOD * D // BLK
MOD_STEPS = NB_MOD // 2
MOD_LATE = 2
MOD_AHEAD = MOD_STEPS - (NB_FF - 1) - MOD_LATE
STREAMS = ((0, 0, CTX), (1, CTX, T))
HALVES = ((0, 320), (320, 640))

V_MODB, V_NORM, V_CONVB, V_CONVC, V_QN, V_KN, V_DN = 0, MODC, MODC + 24, MODC + 30, MODC + 48, MODC + 49, MODC + 50
V_ROWS = MODC + 51

C_QA, C_KA, C_VA, C_GB, C_GC, C_XB, C_QC, C_KC, C_VC, C_ZC, C_XD = 0, 2, 3, 4, 6, 8, 10, 12, 14, 16, 18
COL_ROWS = 2304
COL_XD = 2320
LEVELS = 7
TT_TILE = LEVELS + 1
YE_TILE = 2 * LEVELS - 3
NORMS = (C_QA, C_QA + 1, C_KA, C_KC, C_KC + 1, C_QC, C_QC + 1)

T_ID, T_ONE, T_MASK, T_NEG, T_TRI, T_SUM, T_BC, T_ROT = 0, 128, 256, 256 + 2 * LEVELS * 128, 0, 0, 0, 0
T_TRI = T_NEG + 256
T_SUM = T_TRI + 256
T_BC = T_SUM + 98
T_ROT = T_BC + 7 * 128
T_SC = T_ROT + 128
T_SEL = T_SC + 2
T_ALL = T_SEL + 2
U_COS, U_SIN, U_DFT, U_CL, U_SL, U_CC, U_SCX = 0, 512, 1024, 1280, 1280 + 2048, 1280 + 4096, 1280 + 4096 + 128
U_ALL = U_SCX + 128

RAW_FF1, RAW_MIX, RAW_FF2, RAW_LAYER = 0, 11, 16, 27
UN_FF1, UN_MIX = 0, 11


def un_ff2(u):
    return 15 if u == 3 else 16


def un_layer(u):
    return un_ff2(u) + NB_FF


OUT_BLOCKS = (1, 1, 2)

ACC_FF1, ACC_PROJ, ACC_OUT, ACC_FF2, ACC_LAYER = 0, 88, 110, 118, 206


class Event:

    def __init__(self, sem, per_layer, credit=0):
        self.sem, self.per_layer, self.credit = sem, per_layer, credit

    def at(self, layer, n):
        return layer * self.per_layer + (n + self.credit)


def build(nc, a, tables, mixer_tables, outs):
    with ExitStack() as ctx:
        ps_all = ctx.enter_context(nc.psum_tensor("ps", [P, 4096], F32))

        place = [((int(nc.sbuf_base) + 63) // 64) * 64]
        made = {}

        def at(name, cols, dt=F32, offset=None):
            off = place[0] if offset is None else offset
            t = nc.alloc_sbuf_tensor_at(name, [P, cols], dt, offset=off)
            if offset is None:
                place[0] = off + (cols * 4 + 31) // 32 * 32
            made[name] = off
            return t

        xT = at("xT", KC * T)[:].rearrange("p (c t) -> p c t", c=KC)
        hh = at("hh", KC * T, F32R)[:].rearrange("p (c t) -> p c t", c=KC)
        hl = at("hl", KC * T, F32R)[:].rearrange("p (c t) -> p c t", c=KC)
        raw = [at(f"raw{s}", 2048)[:] for s in range(3)]
        un = [(at(f"uh{u}", 1024, F32R)[:], at(f"ul{u}", 1024, F32R)[:]) for u in range(6)]
        arena0 = made["uh0"]
        PTt = at("PT", 21 * T)
        PT = PTt[:].rearrange("p (c t) -> p c t", c=21)
        pt0 = made["PT"]
        gh = at("gh", 4 * T, F32R, pt0)[:].rearrange("p (g t) -> p g t", g=4)
        gl = at("gl", 4 * T, F32R, pt0 + 4 * T * 4)[:].rearrange("p (g t) -> p g t", g=4)
        PS = PT[:, 20, :]
        tb = at("tb", T_ALL)[:]
        vrow = at("vrow", 128)[:]
        vcol = at("vcol", 128)[:]
        condP = at("condP", KC * 32)[:].rearrange("p (k m) -> p k m", k=KC)
        condE = at("condE", 16)[:]
        fcol = at("fcol", 8)[:]
        modT = at("modT", MODC * 2)[:].rearrange("p (c s) -> p c s", s=2)
        mA = at("mA", 48)[:].rearrange("p (n c s) -> p n c s", n=3, c=KC)
        ast = at("ast", 16)[:]
        gsm = at("gsm", 400)[:]
        adt = at("adt", 4)[:]
        assert place[0] <= int(nc.sbuf_usable_end), (place[0], nc.sbuf_usable_end)

        def ar(name, off, cols):
            assert off + cols <= 12288
            return at(name, cols, F32, arena0 + 4 * off)[:]

        ub = ar("ub", 0, U_ALL)
        A0 = U_ALL
        sq7 = ar("sq7", A0, 7 * T).rearrange("p (c t) -> p c t", c=7)
        cv = ar("cv", A0 + 7 * T, 2 * T).rearrange("p (b t) -> p b t", b=2)
        rrow = cv
        xcs = at("xcs", 5 * 256, F32, made["hh"] + 4 * T * 4)[:].rearrange("p (t n) -> p t n", t=5)
        kall = ar("kall", A0 + 1280, T)
        vtok = ar("vtok", A0 + 1920, 6 * 128).rearrange("p (t n) -> p t n", t=6)
        pexp = ar("pexp", A0 + 2688, 2 * T).rearrange("p (b t) -> p b t", b=2)
        pTs = ar("pTs", A0 + 3968, T).rearrange("p (k n) -> p k n", k=5)
        qs = ar("qs", A0 + 4608, 256).rearrange("p (c t) -> p c t", c=2)
        ckr = ar("ckr", A0 + 4864, 128)
        kct = ar("kct", A0 + 4992, 128)
        rtmp = ar("rtmp", A0 + 5120, 512)
        def dn(name, off, d, cols):
            return ar(f"{name}{d}", d * 6144 + off, cols)
        dd = []
        for d in range(2):
            f4 = lambda n, o: dn(n, o, d, 512).rearrange("p (h t) -> p h t", h=4)
            f2 = lambda n, o: dn(n, o, d, 256).rearrange("p (c t) -> p c t", c=2)
            dd.append(dict(E=f4("dE", 0), AQ=f4("dAQ", 512), LT=f4("dLT", 1024), B0=f4("dB0", 1536), B1=f4("dB1", 2048),
                           Y=f4("dY", 2560), T=f4("dT", 3072), TT=f4("dTT", 3584), kbg=f2("dkbg", 4096), vb=f2("dvb", 4352),
                           kdec=f2("dkdec", 4608), nwT=f2("dnwT", 4864), vnew=f2("dvnew", 5120), qg=f2("dqg", 5376),
                           kbT=f2("dkbT", 5632), kst=f2("dkst", 5888)))
            dd[d]["qst"] = f2("dqst", 2048)

        oC = PT[:, 0:2, :]
        ktok = PT[:, 4:6, :].rearrange("p c (t n) -> p c t n", t=NT)
        vtokc = PT[:, 6:8, :].rearrange("p c (t n) -> p c t n", t=NT)
        gcr = PT[0:8, 8, :]
        er = PT[0:8, 9, :]
        Sctx = PT[:, 2, 0:512].rearrange("p (d c n) -> p d c n", d=2, c=2)
        Slat = PT[:, 3, 0:512].rearrange("p (d c n) -> p d c n", d=2, c=2)
        sqr = PT[:, 10:12, :]
        rt = PT[:, 10, :]
        ssum = PT[:, 20, :]
        t1 = PT[:, 8:10, :]
        mraw = [PTt[:, 12 * T + 2048 * m:12 * T + 2048 * (m + 1)].rearrange("p (k n) -> p k n", k=KC) for m in range(2)]
        mrow = PTt[:, 12 * T + 4096:12 * T + 4608].rearrange("p (m n) -> p m n", m=2)
        sil = PT[:, 8:10, :]
        gf = PT[:, 10:12, :]

        gk = lambda i: gsm[:, 40 * i:40 * i + 40].rearrange("p (t e) -> p t e", t=NT)
        G_BETA, G_G, G_GC, G_EG, G_BG, G_KD, G_EGL, G_T = range(8)

        def tcol(c, n=128):
            return tb[:, c:c + n]
        ident, ones = tcol(T_ID), tcol(T_ONE)
        mask = lambda d, lv: tcol(T_MASK + (d * LEVELS + lv) * 128)
        negm = lambda d: tcol(T_NEG + 128 * d)
        tri = lambda d: tcol(T_TRI + 128 * d)

        def bank(b, n=512, at=0):
            return ps_all[:, b * 512 + at:b * 512 + at + n]

        def pair(q):
            return ps_all[:, q * 1024 + 192:q * 1024 + 832]

        def tiles5(b):
            return ps_all[:, b * 512 + 384:b * 512 + 1024].rearrange("p (t n) -> p t n", t=5)

        mod_rows = ps_all[:, 4 * 512:6 * 512].rearrange("p (m n) -> p m n", m=2)[:, :, 0:BLK]
        mod_cols = bank(7, 8)

        def S(name):
            return ctx.enter_context(nc.semaphore(name))

        def ev(name, per_layer, credit=0):
            return Event(S(name), per_layer, credit)

        raw_full = [S(f"raw_full{s}") for s in range(3)]
        raw_free = [ev(f"raw_free{s}", RAW_LAYER, 1) for s in range(3)]
        hi_done = [ev(f"hi_done{u}", un_layer(u)) for u in range(6)]
        split_full = [ev(f"split_full{u}", un_layer(u)) for u in range(6)]
        unit_done = [ev(f"unit_done{u}", un_layer(u), 1) for u in range(6)]
        acc_used = ev("acc_used", ACC_LAYER, 2)
        y_done = ev("y_done", 14 * NB_FF)
        tables_in, x_in, vec_in, out_done, st_in = S("tables_in"), S("x_in"), S("vec_in"), S("out_done"), S("st_in")
        xt_done, xt_used, cond_done, cond_exp, cond_ready = S("xt_done"), S("xt_used"), S("cond_done"), S("cond_exp"), S("cond_ready")
        vec_zero, settled = S("vec_zero"), S("settled")
        vecT_done, x_ready = ev("vecT_done", 1), S("x_ready")
        mod_full = [S(f"mod_full{m}") for m in range(2)]
        mod_free = [ev(f"mod_free{m}", MOD_STEPS, 1) for m in range(2)]
        mrow_ready, mcol_done, mcol_used = ev("mrow_ready", MOD_STEPS), ev("mcol_done", MOD_STEPS, 1), ev("mcol_used", MOD_STEPS, 1)
        sq_ready, sum_ready, ss_done, rt_ready = ev("sq_ready", 24), ev("sum_ready", 18), ev("ss_done", 3), ev("rt_ready", 6)
        t1_ready, hh_ready, h_ready = ev("t1_ready", 24), ev("hh_ready", 24), ev("h_ready", 24)
        sil_ready, gf_ready, gh_ready, g_ready = (ev(n, 4 * NB_FF) for n in ("sil_ready", "gf_ready", "gh_ready", "g_ready"))
        proj_done = ev("proj_done", 1)
        mt_in, dft_in, ft_in = ev("mt_in", 16 * 5), ev("dft_in", 16), ev("ft_in", 16)
        cv_ready, cv_used = ev("cv_ready", 6), ev("cv_used", 6)
        ob_ready, ob_hi = ev("ob_ready", 1), ev("ob_hi", 1)
        sq7_ready, nr_done, nq_ready, nrow_ready = (ev(n, 2) for n in ("sq7_ready", "nr_done", "nq_ready", "nrow_ready"))
        bc_done, bc_used = ev("bc_done", 9), ev("bc_used", 9)
        tr_done, tr_used, rot_done, roped = ev("tr_done", 1), ev("tr_used", 1), ev("rot_done", 3), ev("roped", 1)
        qs_ready = ev("qs_ready", 5)
        s_done, nmax_ready, p_exp, p_ready, pT_done, pT_used, pv_done = (ev(n, 20) for n in ("s_done", "nmax_ready", "p_exp", "p_ready", "pT_done", "pT_used", "pv_done"))
        pv_used = ev("pv_used", 10)
        f1_done, f1_used, f2_done, f_hi, f_lo = (ev(n, 2) for n in ("f1_done", "f1_used", "f2_done", "f_hi", "f_lo"))
        e_rows, rows_ready, e_ln = ev("e_rows", 1), ev("rows_ready", 1), ev("e_ln", 1)
        sp_x = ev("sp_x", 1)
        gt_done, gt_used, gc_done, gc_ready, gexp_ready, gcol_ready = (ev(n, 1) for n in ("gt_done", "gt_used", "gc_done", "gc_ready", "gexp_ready", "gcol_ready"))
        gr_done, gr_used, kv_done, kv_used = ev("gr_done", 1), ev("gr_used", 1), ev("kv_done", 4), ev("kv_used", 4)
        oz_ready = ev("oz_ready", 1)
        dv = [dict((n, ev(f"{n}{d}", k * NT)) for n, k in (
            ("bcast", 1), ("diff", 1), ("decay", 1), ("staged", 1), ("gram", 1), ("lt", 1), ("bm", LEVELS), ("b1", 1), ("tt", TT_TILE),
            ("y", LEVELS - 1), ("ye", YE_TILE), ("p1", LEVELS - 2), ("p2", LEVELS - 1), ("kb", 1),
            ("wt", 1), ("wte", 1), ("vn", 1), ("vne", 1), ("os", 1), ("ose", 1))) for d in range(2)]
        st_out = ev("st_out", 16 * 4)
        oc_ready, oc_gate, oc_hi, oc_lo = ev("oc_ready", 1), ev("oc_gate", 1), ev("oc_hi", 1), ev("oc_lo", 1)
        kv_out = ev("kv_out", 32)
        fin_x, fin_t, fin_e = S("fin_x"), S("fin_t"), S("fin_e")

        block = ctx.enter_context(nc.Block())

        xrow = PTt[:, 0:NT * D].rearrange("p (t n) -> p t n", t=NT)
        fin_row = PTt[:, NT * D:2 * NT * D].rearrange("p (t n) -> p t n", t=NT)

        def raw_view(s, c, kind):
            if kind == "heads":
                return raw[s].rearrange("p (k g c n) -> p k g c n", k=KC, g=2, c=2)[:, :, :, c, :]
            if kind == "rows":
                return raw[s][:, c * 1024:(c + 1) * 1024]
            return raw[s].rearrange("p (k n) -> p k n", k=KC)[:, :, c * P:(c + 1) * P]

        def settle(eng):
            eng.sem_inc(settled, 1)

        def raw_count(l, s, use, extra=0):
            return l * (32 * RAW_LAYER + 16 * OUT_BLOCKS[s]) + (32 * (use + 1) + 16 * extra)

        def un_view(u, kind):
            if kind == "heads":
                return u.rearrange("p (k g n) -> p k g n", k=KC, g=2)
            return u if kind == "rows" else u.rearrange("p (k n) -> p k n", k=KC)

        @block.sync
        def _(sp):
            sp.dma_start(tb, tables).then_inc(tables_in, 16)
            sp.dma_start(xrow[:, 0, :], a["x_prompt"][0]).then_inc(x_in, 16)
            sp.dma_start(xrow[:, 1:NT, :], a["x_sample"][0].rearrange("(t p) n -> p t n", p=P)).then_inc(x_in, 16)
            for s in range(3):
                sp.sem_inc(raw_free[s].sem, 1)
            for m in range(2):
                sp.sem_inc(mod_free[m].sem, 1)

            def load(l, s, use, first, second):
                sp.wait_ge(raw_free[s].sem, raw_free[s].at(l, use))
                for dst, src in (first, second):
                    sp.dma_start(dst, src).then_inc(raw_full[s], 16)

            def load_cols(l, s, use, w, col):
                r = raw[s].rearrange("p (k n) -> p k n", k=KC)
                v = w.rearrange("(k p) n -> p k n", p=P)[:, :, bass.ds(col, BLK)]
                load(l, s, use, (r[:, 0:4, :], v[:, 0:4, :]), (r[:, 4:8, :], v[:, 4:8, :]))

            def load_mod(l, m, use, block):
                sp.wait_ge(mod_free[m].sem, mod_free[m].at(l, use))
                v = a["mod_w"][bass.ds(l, 1)].rearrange("o (k p) n -> (o p) k n", p=P)
                sp.dma_start(mraw[m], v[:, :, bass.ds(block * BLK, BLK)]).then_inc(mod_full[m], 16)

            def load_up(l, i, w1, w3, base):
                load_cols(l, 0, base + i, w1, i * BLK)
                load_cols(l, 1, base + i, w3, i * BLK)

            def load_down(l, i, w2, base):
                r = raw[2].rearrange("p (k n) -> p k n", k=2)
                v = w2[bass.ds(i * BLK, BLK), :].rearrange("(k p) n -> p k n", p=P)
                load(l, 2, base + i, (r[:, 0, :], v[:, 0, :]), (r[:, 1, :], v[:, 1, :]))

            with sp.Fori(0, DEPTH) as l:
                def w(name):
                    return a[name][bass.ds(l, 1)].rearrange("o k n -> (o k) n")
                load_up(l, 0, w("ffn1_w1"), w("ffn1_w3"), RAW_FF1)
                with sp.Fori(0, MOD_AHEAD) as i:
                    for m in range(2):
                        load_mod(l, m, i, 2 * i + m)
                load_down(l, 0, w("ffn1_w2"), RAW_FF1)
                with sp.Fori(1, NB_FF) as i:
                    load_up(l, i, w("ffn1_w1"), w("ffn1_w3"), RAW_FF1)
                    for m in range(2):
                        load_mod(l, m, i + (MOD_AHEAD - 1), 2 * i + (2 * (MOD_AHEAD - 1) + m))
                    load_down(l, i, w("ffn1_w2"), RAW_FF1)
                win = w("w_in")
                for j in range(10):
                    s, use = j % 3, RAW_MIX + j // 3
                    load_cols(l, s, use, win, COL_XD if j == 9 else j * BLK)
                r = raw[1].rearrange("p (k n) -> p k n", k=KC)
                v = win.rearrange("(k p) n -> p k n", p=P)
                load(l, 1, RAW_MIX + 3, (r[:, :, 0:8], v[:, :, COL_ROWS:COL_ROWS + 8]),
                     (r[:, :, 32:40], v[:, :, COL_ROWS + 8:COL_ROWS + 16]))
                wout = w("w_out")
                for j in range(4):
                    s = (2, 0, 1, 2)[j]
                    use = RAW_MIX + (3, 4, 4, 4)[j]
                    r = raw[s].rearrange("p (k n) -> p k n", k=KC)
                    cols = wout[:, j * BLK:(j + 1) * BLK]
                    sp.wait_ge(raw_free[s].sem, raw_free[s].at(l, use))
                    for c in range(2):
                        sp.dma_start(r[:, c, :], cols[0:256, :].rearrange("(g c q) n -> c g q n", g=2, c=2)[c]).then_inc(raw_full[s], 16)
                    sp.dma_start(r[:, 2:8, :], cols.rearrange("(k p) n -> p k n", p=P)[:, 2:8, :]).then_inc(raw_full[s], 16)
                load_up(l, 0, w("ffn2_w1"), w("ffn2_w3"), RAW_FF2)
                sp.wait_ge(oc_lo.sem, oc_lo.at(l, 1))
                for n in range(MOD_STEPS - MOD_LATE, MOD_STEPS):
                    for m in range(2):
                        load_mod(l, m, n, 2 * n + m)
                load_down(l, 0, w("ffn2_w2"), RAW_FF2)
                with sp.Fori(1, NB_FF) as i:
                    load_up(l, i, w("ffn2_w1"), w("ffn2_w3"), RAW_FF2)
                    load_down(l, i, w("ffn2_w2"), RAW_FF2)

            sp.wait_ge(fin_e, 2)
            sp.dma_start(outs[0][0], fin_row[:, 0, :]).then_inc(out_done, 16)
            for t in range(1, NT):
                sp.wait_ge(fin_e, 2 * t + 2)
                sp.dma_start(outs[1][0, (t - 1) * P:t * P, :], fin_row[:, t, :]).then_inc(out_done, 16)
            sp.wait_ge(out_done, 16 * NT)

        @block.gpsimd
        def _(pool):
            pool.memset(vrow, 0.0)
            pool.drain().then_inc(vec_zero, 1)
            pool.wait_ge(vec_zero, 1)
            pool.dma_start(vrow[0:8, :], a["c_ctx"].rearrange("(k p) -> k p", p=P)).then_inc(st_in, 16)
            pool.dma_start(vrow[8:16, :], a["c"][0].rearrange("(k p) -> k p", p=P)).then_inc(st_in, 16)
            pool.dma_start(vrow[16:24, :], a["final_norm"].rearrange("(k p) -> k p", p=P)).then_inc(st_in, 16)
            pool.memset(condP, 0.0)
            pool.drain().then_inc(vec_zero, 1)

            def sums(l, st):
                for c in range(1, KC - 1):
                    pool.wait_ge(sq_ready.sem, sq_ready.at(l, 8 * st + c + 1))
                    pool.tensor_tensor(ssum, sqr[:, 0, :] if c == 1 else ssum, sqr[:, c % 2, :], ALU.add).then_inc(sum_ready.sem, 1)
                    pool.drain()
            pool.wait_ge(cond_ready, 1)
            with pool.Fori(0, DEPTH) as l:
                one = bass.ds(l, 1)

                def vec(row, n, src):
                    pool.dma_start(vrow[row:row + n, :], src).then_inc(vec_in, 16)
                vecT_done_prev = l * 1 + 1
                pool.wait_ge(cond_ready, vecT_done_prev)
                vec(V_MODB, MODC, a["mod_b"][one].rearrange("o (k p) -> (o k) p", p=P))
                for n, name in enumerate(("norm_ffn1", "norm_mix", "norm_ffn2")):
                    vec(V_NORM + 8 * n, 8, a[name][one].rearrange("o (k p) -> (o k) p", p=P))
                vec(V_CONVB, 6, a["conv_b_w"][one].rearrange("o j (k p) -> (o j k) p", p=P))
                vec(V_CONVC, 18, a["conv_c_w"][one].rearrange("o j (k p) -> (o j k) p", p=P))
                for v, name in ((V_QN, "q_norm"), (V_KN, "k_norm"), (V_DN, "delta_norm")):
                    for g in range(2):
                        pool.dma_start(vrow[v:v + 1, g * HEAD:(g + 1) * HEAD], a[name][one]).then_inc(vec_in, 16)

                sums(l, 0)
                sums(l, 1)
                pool.wait_ge(proj_done.sem, proj_done.at(l, 1))
                settle(pool)
                for lo, hi, there in ((U_DFT, U_CL, dft_in), (U_CL, U_ALL, ft_in), (0, U_DFT, mt_in)):
                    pool.dma_start(ub[:, lo:hi], mixer_tables[:, lo:hi]).then_inc(there.sem, 16)
                for g, name in enumerate(("delta_a_log", "delta_dt_bias")):
                    pool.dma_start(adt[32:40, g:g + 1], a[name][one].rearrange("o d (h u) -> (o d h) u", u=1)).then_inc(mt_in.sem, 16)
                pool.wait_ge(bc_used.sem, bc_used.at(l, 7))
                settle(pool)
                pool.dma_start(ckr.rearrange("p (h n) -> p h n", h=2),
                               a["cache_k"][0, one].rearrange("o h t n -> (o t) h n")).then_inc(mt_in.sem, 16)
                pool.dma_start(vtok[:, 0, :].rearrange("p (h n) -> p h n", h=2),
                               a["cache_v"][0, one].rearrange("o h t n -> (o t) h n")).then_inc(mt_in.sem, 16)
                pool.wait_ge(tr_used.sem, tr_used.at(l, 1))
                settle(pool)
                pool.dma_start(outs[2][0, one].rearrange("o h t n -> (o t) h n"),
                               kct.rearrange("p (h n) -> p h n", h=2)).then_inc(kv_out.sem, 16)
                pool.dma_start(outs[3][0, one].rearrange("o h t n -> (o t) h n"),
                               vtok[:, 5, :].rearrange("p (h n) -> p h n", h=2)).then_inc(kv_out.sem, 16)
                pool.wait_ge(kv_out.sem, kv_out.at(l, 32))
                pool.wait_ge(pv_done.sem, pv_done.at(l, 20))
                pool.wait_ge(roped.sem, roped.at(l, 1))
                settle(pool)
                pool.memset(PT[:, 2:4, 0:512], 0.0)
                pool.memset(oC, 0.0)
                pool.drain().then_inc(oz_ready.sem, 1)
                pool.wait_ge(oz_ready.sem, oz_ready.at(l, 1))
                settle(pool)
                for c in range(2):
                    for g in range(2):
                        pool.dma_start(Slat[64 * g:64 * g + 64, :, c, 64 * g:64 * g + 64],
                                       a["state_delta"][0, one, :, 2 * c + g].rearrange("o d k v -> (o k) d v")).then_inc(st_in, 16)

                def tile(n):
                    for lv in range(LEVELS):
                        for d in range(2):
                            b, e = dd[d], dv[d]
                            if lv == 0:
                                pool.wait_ge(e["lt"].sem, e["lt"].at(l, n + 1))
                            if lv >= 3:
                                pool.wait_ge(e["y"].sem, e["y"].at(l, (LEVELS - 1) * n + lv - 2))
                            if lv == 2:
                                pool.wait_ge(e["tt"].sem, e["tt"].at(l, TT_TILE * n + 2))
                            pool.tensor_tensor(b["B0" if lv % 2 == 0 else "B1"], b["LT"],
                                               mask(d, lv).rearrange("p (o n) -> p o n", o=1).to_broadcast([P, 4, 128]),
                                               ALU.mult).then_inc(e["bm"].sem, 1)
                tile(0)
                for d in range(2):
                    pool.wait_ge(dv[d]["ose"].sem, dv[d]["ose"].at(l, 1))
                settle(pool)
                for c in range(2):
                    for g in range(2):
                        pool.dma_start(outs[4][0, one, :, 2 * c + g].rearrange("o d k v -> (o k) d v"),
                                       Sctx[64 * g:64 * g + 64, :, c, 64 * g:64 * g + 64]).then_inc(st_out.sem, 16)
                with pool.Fori(1, NT) as i:
                    tile(i)
                pool.wait_ge(st_out.sem, st_out.at(l, 64))
                sums(l, 2)
            sums(DEPTH, 0)

        @block.tensor
        def _(pe):
            def fp32(out, lhsT, rhs, start=True, stop=True, loose=False):
                return pe.matmul(out, lhsT, rhs, start=start, stop=stop, skip_group_check=loose)

            def chunk_product(q, u, ks, first_k=None, start=True, stop=True, rhs=None, wait_k=None):
                wh, wl = un[u]
                last = None
                n = len(ks)
                for i, (wk, mk) in enumerate(ks):
                    if wait_k:
                        wait_k(mk)
                    mh, ml = rhs
                    for p_, (wt, mv) in enumerate(((wh, mh), (wh, ml), (wl, mh))):
                        for lo, hi in HALVES:
                            last = pe.matmul(pair(q)[:, lo:hi], wt[:, wk * P:(wk + 1) * P], mv(mk, lo, hi),
                                             start=start and i == 0 and p_ == 0, stop=stop and i == n - 1 and p_ == 2)
                return last

            h_rhs = (lambda k, lo, hi: hh[:, k, lo:hi], lambda k, lo, hi: hl[:, k, lo:hi])
            k8 = [(k, k) for k in range(KC)]

            def square_sums(l, st):
                pe.wait_ge(sum_ready.sem, sum_ready.at(l, 6 * st + 6))
                for lo, hi in HALVES:
                    fp32(pair(0)[:, lo:hi], ones, ssum[:, lo:hi], True, False)
                pe.wait_ge(sq_ready.sem, sq_ready.at(l, 8 * st + 8))
                for lo, hi in HALVES:
                    mm = fp32(pair(0)[:, lo:hi], ones, sqr[:, 1, lo:hi], False, True)
                mm.then_inc(ss_done.sem, 1)

            def modulation_rows(l, n):
                for m in range(2):
                    pe.wait_ge(mod_full[m], l * (16 * MOD_STEPS) + 16 * (n + 1))
                    for k in range(KC):
                        g = 32 * (k % 4)
                        mm = pe.matmul(mod_rows[g:g + 32, m, :], condP[:, k, :], mraw[m][:, k, :],
                                       start=k < 4, stop=k >= 4, skip_group_check=True)
                    mm.then_inc(mod_free[m].sem, 1)

            def modulation_cols(l, n):
                pe.wait_ge(mrow_ready.sem, mrow_ready.at(l, n + 1))
                pe.wait_ge(mcol_used.sem, mcol_used.at(l, n))
                for m in range(2):
                    for c in range(2):
                        mm = fp32(mod_cols[:, 4 * m + 2 * c:4 * m + 2 * c + 2], mrow[:, m, c * P:(c + 1) * P], tcol(T_SEL, 2))
                mm.then_inc(mcol_done.sem, 1)

            def feed_forward(l, f):
                ubase = [0] * 6 if f == 0 else [un_ff2(u) for u in range(6)]
                st = 0 if f == 0 else 2
                abase = ACC_FF1 if f == 0 else ACC_FF2

                def up(i, c):
                    for w in range(2):
                        u = 2 * w + c
                        pe.wait_ge(split_full[u].sem, split_full[u].at(l, ubase[u] + i + 1))
                        n = 2 * NB_FF * f + 2 * i + c
                        ev_ = sil_ready if w == 0 else gf_ready
                        pe.wait_ge(ev_.sem, ev_.at(l, n))
                        chunk_product(w, u, k8, rhs=h_rhs).then_inc(unit_done[u].sem, 1)

                def up_first():
                    for u in range(4):
                        pe.wait_ge(split_full[u].sem, split_full[u].at(l, ubase[u] + 1))
                    for k in range(KC):
                        pe.wait_ge(h_ready.sem, h_ready.at(l, 8 * st + k + 1))
                        for c in range(2):
                            for w in range(2):
                                mm = chunk_product(2 * c + w, 2 * w + c, [(k, k)], rhs=h_rhs, start=k == 0, stop=k == KC - 1)
                                if k == KC - 1:
                                    mm.then_inc(unit_done[2 * w + c].sem, 1)

                def down(i, n=None):
                    par = 2 * (i % 2)
                    for g in range(2):
                        pe.wait_ge(g_ready.sem, g_ready.at(l, 2 * NB_FF * f + 2 * i + g + 1))
                        pe.wait_ge(split_full[4 + g].sem, split_full[4 + g].at(l, ubase[4 + g] + i + 1))
                    for o in range(KC):
                        if o == 1 and n is not None:
                            pe.wait_ge(mcol_used.sem, mcol_used.at(l, n + 1))
                        pe.wait_ge(acc_used.sem, acc_used.at(l, abase + 8 * i + o - 1))
                        for g in range(2):
                            rhs = (lambda k, lo, hi: gh[:, bass.ds(par + k, 1), lo:hi].rearrange("p o t -> p (o t)"),
                                   lambda k, lo, hi: gl[:, bass.ds(par + k, 1), lo:hi].rearrange("p o t -> p (o t)"))
                            mm = chunk_product(2 + o % 2, 4 + g, [(o, g)], start=g == 0, stop=g == 1, rhs=rhs)
                            if o == KC - 1:
                                mm.then_inc(unit_done[4 + g].sem, 1)
                        if o < KC - 1:
                            mm.then_inc(y_done.sem, 1)
                up_first()
                with pe.Fori(1, NB_FF) as i:
                    up(i, 0)
                    n = i + (MOD_AHEAD - 1)
                    if f == 0:
                        pe.wait_ge(acc_used.sem, acc_used.at(l, abase + 8 * i - 8))
                        modulation_rows(l, n)
                    up(i, 1)
                    if f == 0:
                        modulation_cols(l, n)
                    down(i - 1, n if f == 0 else None)
                down(NB_FF - 1)
                square_sums(l, 1 if f == 0 else 3)

            pe.wait_ge(tables_in, 16)
            pe.wait_ge(x_in, 32)
            n = 0
            for t in range(NT):
                for q in range(2):
                    b = n % 4
                    if n >= 4:
                        pe.wait_ge(xt_used, n - 3)
                    for c in range(4):
                        mm = pe.transpose(bank(b, 128, c * 128), xrow[:, t, (4 * q + c) * P:(4 * q + c + 1) * P], ident)
                    mm.then_inc(xt_done, 1)
                    n += 1
            pe.wait_ge(st_in, 48)
            pe.transpose(bank(4, 128), vrow, ident).then_inc(cond_done, 1)
            pe.wait_ge(cond_ready, 1)
            for u in range(6):
                pe.sem_inc(unit_done[u].sem, 1)
            pe.wait_ge(xt_used, 10)
            square_sums(0, 0)

            with pe.Fori(0, DEPTH) as l:
                pe.wait_ge(vec_in, 16 * 12 * (l + 1))
                pe.wait_ge(acc_used.sem, acc_used.at(l, 0))
                pe.transpose(bank(6, 128), vrow, ident).then_inc(vecT_done.sem, 1)
                with pe.Fori(0, MOD_AHEAD) as i:
                    modulation_rows(l, i)
                    modulation_cols(l, i)
                feed_forward(l, 0)

                def project(q, s, c, use):
                    u = 2 * s + c
                    pe.wait_ge(split_full[u].sem, split_full[u].at(l, UN_MIX + use + 1))
                    pe.wait_ge(acc_used.sem, acc_used.at(l, ACC_PROJ + q - 1))
                    chunk_product(2 + c, u, k8, rhs=h_rhs).then_inc(unit_done[u].sem, 1)
                for c in range(2):
                    pe.wait_ge(split_full[c].sem, split_full[c].at(l, UN_MIX + 1))
                for k in range(KC):
                    pe.wait_ge(h_ready.sem, h_ready.at(l, 8 + k + 1))
                    for c in range(2):
                        mm = chunk_product(2 + c, c, [(k, k)], rhs=h_rhs, start=k == 0, stop=k == KC - 1)
                        if k == KC - 1:
                            mm.then_inc(unit_done[c].sem, 1)
                for s in range(1, 3):
                    for c in range(2):
                        project(2 * s + c, s, c, 0)
                with pe.Fori(1, 3) as i:
                    for s in range(3):
                        for c in range(2):
                            project(6 * i + (2 * s + c), s, c, i)
                for c in range(2):
                    project(18 + c, 0, c, 3)
                project(20, 1, 0, 3)

                def head_norm_rows(k, chunks):
                    pe.wait_ge(sq7_ready.sem, sq7_ready.at(l, k + 1))
                    for lo, hi in HALVES:
                        for c in range(chunks):
                            mm = fp32(pair(0)[0:14, lo:hi], tb[:, T_SUM + 14 * c:T_SUM + 14 * c + 14],
                                      (sq7 if k == 0 else PT[:, 4:6, :])[:, c, lo:hi], c == 0, c == chunks - 1)
                    mm.then_inc(nr_done.sem, 1)

                def head_norm_spread(k, chunks):
                    pe.wait_ge(nrow_ready.sem, nrow_ready.at(l, k + 1))
                    for c in range(chunks):
                        n = 7 * k + c
                        if c >= 2:
                            pe.wait_ge(bc_used.sem, bc_used.at(l, n - 1))
                        for lo, hi in HALVES:
                            mm = fp32(pair(c % 2)[:, lo:hi], tb[0:14, T_BC + 128 * c:T_BC + 128 * c + 128],
                                      rrow[0:14, 0, lo:hi] if k == 0 else PT[0:14, 8, lo:hi])
                        mm.then_inc(bc_done.sem, 1)
                def fourier_features(c):
                    if c:
                        pe.wait_ge(f_lo.sem, f_lo.at(l, c))
                    for t in range(NT):
                        mm = fp32(ps_all[:, 2816 + t * 256:2816 + (t + 1) * 256], PT[:, C_XD + c, t * P:(t + 1) * P], ub[:, U_DFT:U_DFT + 256])
                    mm.then_inc(f1_done.sem, 1)

                def fourier_tokens(c):
                    pe.wait_ge(f1_used.sem, f1_used.at(l, c + 1))
                    fp32(bank(4, 128, 384), xcs[:, 0, 0:128], ub[:, U_CC:U_CC + 128], True, False)
                    fp32(bank(4, 128, 384), xcs[:, 0, 128:256], ub[:, U_SCX:U_SCX + 128], False, True)
                    for t in range(1, NT):
                        for g in range(2):
                            u0 = (U_CL, U_SL)[g] + (t - 1) * 512
                            mm = fp32(bank(5), xcs[:, t, g * 128:(g + 1) * 128], ub[:, u0:u0 + 512], t == 1 and g == 0, t == NT - 1 and g == 1)
                    mm.then_inc(f2_done.sem, 1)
                pe.wait_ge(proj_done.sem, proj_done.at(l, 1))
                pe.wait_ge(dft_in.sem, dft_in.at(l, 16))
                fourier_features(0)
                pe.wait_ge(ft_in.sem, ft_in.at(l, 16))
                fourier_tokens(0)
                head_norm_rows(0, 7)
                fourier_features(1)
                head_norm_spread(0, 7)
                fourier_tokens(1)

                pe.wait_ge(bc_used.sem, bc_used.at(l, 7))
                pe.wait_ge(mt_in.sem, mt_in.at(l, 80))
                for t in range(1, NT):
                    pe.transpose(bank(0, 128, (t - 1) * 128), PT[:, C_VA, t * P:(t + 1) * P], ident)
                pe.transpose(bank(1, 128, 0), PT[:, C_VA, 0:P], ident)
                pe.transpose(bank(1, 128, 128), PT[:, C_KA, 0:P], ident)
                pe.transpose(bank(1, 128, 256), ckr, ident).then_inc(tr_done.sem, 1)
                for n, c in enumerate((C_QA, C_QA + 1, C_KA)):
                    fp32(bank((2, 3, 6)[n]), tcol(T_ROT), PT[:, c, CTX:T]).then_inc(rot_done.sem, 1)
                pe.wait_ge(f_lo.sem, f_lo.at(l, 2))
                pe.wait_ge(roped.sem, roped.at(l, 1))
                pe.wait_ge(tr_used.sem, tr_used.at(l, 1))

                def attend(n, latent, part="whole"):
                    def scores(k, n=n):
                        c, g = k // 2, k % 2
                        if k == 0:
                            pe.wait_ge(qs_ready.sem, qs_ready.at(l, n + 1))
                        if k >= 2 or latent:
                            pe.wait_ge(p_exp.sem, p_exp.at(l, 4 * n + (k - 1)))
                        lhs = qs[64 * g:64 * g + 64, c, :]
                        if latent:
                            for lo, hi in HALVES:
                                mm = fp32(pair(k % 2)[:, lo:hi], lhs, kall[64 * g:64 * g + 64, lo:hi])
                        else:
                            mm = fp32(pair(k % 2)[:, 0:P], lhs, PT[64 * g:64 * g + 64, C_KA, 0:P])
                        mm.then_inc(s_done.sem, 1)

                    def turn(k):
                        pe.wait_ge(p_ready.sem, p_ready.at(l, 4 * n + k + 1))
                        if k >= 1:
                            pe.wait_ge(pT_used.sem, pT_used.at(l, 4 * n + k))
                        for t in range(5 if latent else 1):
                            mm = pe.transpose(tiles5(4)[:, t, :], pexp[:, k % 2, t * P:(t + 1) * P], ident)
                        mm.then_inc(pT_done.sem, 1)

                    def values(k):
                        c, g = k // 2, k % 2
                        pe.wait_ge(pT_used.sem, pT_used.at(l, 4 * n + k + 1))
                        if latent and g == 0:
                            pe.wait_ge(pv_used.sem, pv_used.at(l, 2 * n + c - 1))
                        for t in range(5 if latent else 1):
                            mm = fp32(ps_all[64 * g:64 * g + 64, (6 + c) * 512:(6 + c) * 512 + 128],
                                      vtok[:, t if latent else 5, 64 * g:64 * g + 64], pTs[:, t, :], t == 0, t == (4 if latent else 0))
                        mm.then_inc(pv_done.sem, 1)
                    if part in ("whole", "first"):
                        scores(0)
                        scores(1)
                    if part == "first":
                        return
                    for k in range(4):
                        turn(k)
                        if k + 2 < 4:
                            scores(k + 2)
                        elif part == "middle":
                            scores(k - 2, n + 1)
                        values(k)
                attend(0, False)
                attend(1, True, "first")
                with pe.Fori(1, NT - 1) as i:
                    attend(i, True, "middle")
                attend(NT - 1, True, "last")

                pe.wait_ge(pv_used.sem, pv_used.at(l, 10))
                pe.wait_ge(rows_ready.sem, rows_ready.at(l, 1))
                pe.wait_ge(f_lo.sem, f_lo.at(l, 2))
                settle(pe)
                for t in range(NT):
                    pe.transpose(bank(0, 8, 8 * t), PS[0:8, t * P:(t + 1) * P], ident[0:8, 0:8])
                for t in range(NT):
                    mm = pe.transpose(bank(2, 8, 8 * t), PS[32:40, t * P:(t + 1) * P], ident[32:40, 32:40])
                mm.then_inc(gt_done.sem, 1)
                for k, (chunk) in enumerate((C_KC, C_KC + 1, C_VC, C_VC + 1)):
                    if k >= 2:
                        pe.wait_ge(kv_used.sem, kv_used.at(l, k - 1))
                    for t in range(NT):
                        mm = pe.transpose(tiles5((4, 6)[k % 2])[:, t, :], PT[:, chunk, t * P:(t + 1) * P], ident)
                    mm.then_inc(kv_done.sem, 1)
                pe.wait_ge(gt_used.sem, gt_used.at(l, 1))
                for d in range(2):
                    fp32(bank(1, 40).rearrange("p (t d h) -> p t d h", t=NT, d=2)[:, :, d, :], tri(d), gk(G_G)[:, :, 4 * d:4 * d + 4])
                fp32(bank(1, 40, 40), ones, gk(G_G)).then_inc(gc_done.sem, 1)
                pe.wait_ge(gc_ready.sem, gc_ready.at(l, 1))
                for t in range(NT):
                    mm = pe.transpose(tiles5(2)[0:8, t, :], gk(G_GC)[:, t, :], ident)
                mm.then_inc(gr_done.sem, 1)
                pe.wait_ge(gr_used.sem, gr_used.at(l, 1))
                pe.wait_ge(gcol_ready.sem, gcol_ready.at(l, 1))
                pe.wait_ge(kv_used.sem, kv_used.at(l, 4))
                pe.wait_ge(oz_ready.sem, oz_ready.at(l, 1))
                pe.wait_ge(st_in, 48 + 64 * (l + 1))
                settle(pe)

                def delta(tiles, n, St):
                    cols = [bass.ds(t * P, P) for t in tiles]
                    h4 = lambda d, b: bank(4 * d + b).rearrange("p (h t) -> p h t", h=4)
                    h2 = lambda d, b: bank(4 * d + b, 256).rearrange("p (c t) -> p c t", c=2)
                    for d in range(2):
                        e = dv[d]
                        for h in range(4):
                            r = 4 * d + h
                            fp32(h4(d, 0)[:, h, :], ident[0:8, r:r + 1].to_broadcast([8, P]), gcr[:, cols[d]])
                        for c in range(2):
                            sel = tb[0:8, T_BC + 128 * (2 * d + c):T_BC + 128 * (2 * d + c) + 128]
                            fp32(bank(4 * d + 1, 128, 128 * c), sel, er[:, cols[d]])
                            mm = fp32(bank(4 * d + 1, 128, 256 + 128 * c), sel, PS[0:8, cols[d]])
                        mm.then_inc(e["bcast"].sem, 1)
                    for d in range(2):
                        b, e = dd[d], dv[d]
                        pe.wait_ge(e["staged"].sem, e["staged"].at(l, n + 1))
                        for h in range(4):
                            g, c = 64 * (h % 2), h // 2
                            fp32(bank(4 * d + 2 + h % 2, P, c * P), b["kst"][g:g + 64, c, :], b["qst"][g:g + 64, c, :])
                            mm = fp32(bank(4 * d + 2 + h % 2, P, 256 + c * P), b["kst"][g:g + 64, c, :], b["kbT"][g:g + 64, c, :])
                        mm.then_inc(e["gram"].sem, 1)
                    for d in range(2):
                        b, e = dd[d], dv[d]
                        pe.wait_ge(e["bm"].sem, e["bm"].at(l, LEVELS * n + 1))
                        pe.wait_ge(e["diff"].sem, e["diff"].at(l, n + 1))
                        for h in range(4):
                            mm = pe.transpose(h4(d, 0)[:, h, :], b["B0"][:, h, :], ident)
                        mm.then_inc(e["b1"].sem, 1)
                    for lv in range(1, LEVELS):
                        for d in range(2):
                            b, e = dd[d], dv[d]
                            pe.wait_ge(e["bm"].sem, e["bm"].at(l, LEVELS * n + lv + 1))
                            pe.wait_ge(e["tt"].sem, e["tt"].at(l, TT_TILE * n + (lv + 1 if lv > 1 else 1)))
                            if lv == 1:
                                pe.wait_ge(e["lt"].sem, e["lt"].at(l, n + 1))
                            for h in range(4):
                                mm = fp32(h4(d, 1)[:, h, :], b["B0" if lv % 2 == 0 else "B1"][:, h, :], b["T"][:, h, :])
                            mm.then_inc(e["y"].sem, 1)
                            if lv > 1:
                                for h in range(4):
                                    mm = pe.transpose(h4(d, 3)[:, h, :], b["T"][:, h, :], ident)
                                mm.then_inc(e["p2"].sem, 1)
                        for d in range(2):
                            b, e = dd[d], dv[d]
                            pe.wait_ge(e["ye"].sem, e["ye"].at(l, YE_TILE * n + (2 * lv - 1)))
                            if lv == 1:
                                pe.wait_ge(e["tt"].sem, e["tt"].at(l, TT_TILE * n + 2))
                            if lv < LEVELS - 1:
                                for h in range(4):
                                    mm = fp32(h4(d, 2)[:, h, :], b["TT"][:, h, :], b["Y"][:, h, :])
                                mm.then_inc(e["p1"].sem, 1)
                            else:
                                for h in range(4):
                                    mm = fp32(h4(d, 3)[:, h, :], b["Y"][:, h, :], b["TT"][:, h, :])
                                mm.then_inc(e["p2"].sem, 1)
                    for d in range(2):
                        b, e = dd[d], dv[d]
                        pe.wait_ge(e["kb"].sem, e["kb"].at(l, n + 1))
                        pe.wait_ge(e["tt"].sem, e["tt"].at(l, TT_TILE * n + TT_TILE))
                        for h in range(4):
                            g, c = 64 * (h % 2), h // 2
                            mm = fp32(h2(d, 0)[g:g + 64, c, :], b["kbg"][:, c, g:g + 64], b["TT"][:, h, :])
                        mm.then_inc(e["wt"].sem, 1)
                    for d in range(2):
                        b, e = dd[d], dv[d]
                        pe.wait_ge(e["wte"].sem, e["wte"].at(l, n + 1))
                        for c in range(2):
                            fp32(h2(d, 1)[:, c, :], b["nwT"][:, c, :], St[:, d, c, :])
                            for g in range(2):
                                mm = fp32(bank(4 * d + 1, 64, 128 * c + 64 * g), b["TT"][:, 2 * c + g, :], b["vb"][:, c, 64 * g:64 * g + 64],
                                          False, True, loose=True)
                        mm.then_inc(e["vn"].sem, 1)
                    for d in range(2):
                        b, e = dd[d], dv[d]
                        pe.wait_ge(e["vne"].sem, e["vne"].at(l, n + 1))
                        for c in range(2):
                            fp32(h2(d, 2)[:, c, :], St[:, d, c, :], b["qg"][:, c, :])
                            for g in range(2):
                                fp32(h2(d, 2)[64 * g:64 * g + 64, c, :], b["vnew"][:, c, 64 * g:64 * g + 64], b["AQ"][:, 2 * c + g, :],
                                     False, True, loose=True)
                        for c in range(2):
                            mm = fp32(h2(d, 3)[:, c, :], b["kdec"][:, c, :], b["vnew"][:, c, :])
                        mm.then_inc(e["os"].sem, 1)
                delta((0, 0), 0, Sctx)
                with pe.Fori(1, NT) as i:
                    delta((i, NT - i), i, Slat)
                for d in range(2):
                    pe.wait_ge(dv[d]["ose"].sem, dv[d]["ose"].at(l, NT))
                def first_out(c, ks, start):
                    u = 4 + c
                    if start:
                        pe.wait_ge(split_full[u].sem, split_full[u].at(l, UN_MIX + 4))
                        pe.wait_ge(acc_used.sem, acc_used.at(l, ACC_OUT + c - 1))
                    return chunk_product(2 + c, u, [(k, k) for k in ks], rhs=h_rhs, start=start, stop=not start)
                head_norm_rows(1, 2)
                first_out(0, (0, 1, 2, 3, 6, 7), True)
                head_norm_spread(1, 2)
                first_out(1, (0, 1, 2, 3, 6, 7), True)

                pe.wait_ge(oc_lo.sem, oc_lo.at(l, 1))
                for c in range(2):
                    first_out(c, (4, 5), False).then_inc(unit_done[4 + c].sem, 1)
                for j in range(1, 4):
                    s, use = (2, 0, 1, 2)[j], (3, 4, 4, 4)[j]
                    for c in range(2):
                        u, o = 2 * s + c, 2 * j + c
                        pe.wait_ge(split_full[u].sem, split_full[u].at(l, UN_MIX + (use - 1 if u == 3 else use) + 1))
                        pe.wait_ge(acc_used.sem, acc_used.at(l, ACC_OUT + o - 1))
                        chunk_product(2 + o % 2, u, k8, rhs=h_rhs).then_inc(unit_done[u].sem, 1)
                square_sums(l, 2)
                pe.wait_ge(acc_used.sem, acc_used.at(l, ACC_OUT + KC))
                for n in range(MOD_STEPS - MOD_LATE, MOD_STEPS):
                    modulation_rows(l, n)
                    modulation_cols(l, n)
                feed_forward(l, 1)

            n = 0
            for t in range(NT):
                for q in range(2):
                    if t == 0:
                        pe.wait_ge(fin_x, 4 * (q + 1))
                    if n >= 4:
                        pe.wait_ge(fin_e, n - 3)
                    for c in range(4):
                        mm = pe.transpose(bank(n % 4, 128, c * 128), xT[:, 4 * q + c, t * P:(t + 1) * P], ident)
                    mm.then_inc(fin_t, 1)
                    n += 1

        @block.scalar
        def _(act):
            def hi_part(l, s, c, use, un_use, kind, extra=0):
                u = 2 * s + c
                act.wait_ge(raw_full[s], raw_count(l, s, use, extra))
                act.wait_ge(unit_done[u].sem, unit_done[u].at(l, un_use))
                act.copy(un_view(un[u][0], kind), raw_view(s, c, kind)).then_inc(hi_done[u].sem, 1)

            def squares(l, st, c):
                if c >= 2:
                    act.wait_ge(sum_ready.sem, sum_ready.at(l, 6 * st + max(c - 2, 1)))
                act.activation(sqr[:, c % 2, :], xT[:, c, :], ACT.Square).then_inc(sq_ready.sem, 1)

            def roots(l, st):
                act.wait_ge(ss_done.sem, ss_done.at(l, st + 1))
                for lo, hi in HALVES:
                    act.activation(rt[:, lo:hi], pair(0)[:, lo:hi], ACT.Sqrt, bias=tb[:, T_SC + 1:T_SC + 2], scale=1.0 / D).then_inc(rt_ready.sem, 1)

            def norm(l, st):
                for c in range(KC):
                    act.wait_ge(t1_ready.sem, t1_ready.at(l, 8 * st + c + 1))
                    for s, lo, hi in STREAMS:
                        mm = act.activation(hh[:, c, lo:hi], t1[:, c % 2, lo:hi], ACT.Identity,
                                            bias=modT[:, 24 * st + c, s:s + 1])
                    mm.then_inc(hh_ready.sem, 1)

            def modulation(l, n):
                act.wait_ge(mod_free[1].sem, mod_free[1].at(l, n + 1))
                act.wait_ge(mcol_done.sem, mcol_done.at(l, n))
                act.copy(mrow, mod_rows).then_inc(mrow_ready.sem, 1)

            def feed_forward(l, f, ahead=None):
                ub_ = [0] * 6 if f == 0 else [un_ff2(u) for u in range(6)]
                rb_ = RAW_FF1 if f == 0 else RAW_FF2

                def hi_w13(i, c):
                    for s in range(2):
                        hi_part(l, s, c, rb_ + i, ub_[2 * s + c] + i, "cols", f * OUT_BLOCKS[s])

                def hi_w2(i):
                    for g in range(2):
                        hi_part(l, 2, g, rb_ + i, ub_[4 + g] + i, "rows", f * OUT_BLOCKS[2])

                def chunk(i, c, more, q=0):
                    n = 2 * NB_FF * f + 2 * i + c
                    act.wait_ge(unit_done[c].sem, unit_done[c].at(l, ub_[c] + i + 1))
                    act.activation(sil[:, c, :], pair(q), ACT.Silu).then_inc(sil_ready.sem, 1)
                    act.wait_ge(gf_ready.sem, gf_ready.at(l, n + 1))
                    act.copy(gh[:, bass.ds(2 * (i % 2) + c, 1), :].rearrange("p o t -> p (o t)"), gf[:, c, :]).then_inc(gh_ready.sem, 1)
                    if f == 0 and c == 0 and not (isinstance(i, int) and i == 0):
                        modulation(l, i + (MOD_AHEAD - 1))
                    if more:
                        hi_w13(i + 1, c)
                norm(l, 0 if f == 0 else 2)
                for c in range(2):
                    chunk(0, c, True, 2 * c)
                with act.Fori(1, NB_FF - 1) as i:
                    hi_w2(i - 1)
                    for c in range(2):
                        chunk(i, c, True)
                hi_w2(NB_FF - 2)
                for c in range(2):
                    chunk(NB_FF - 1, c, False)
                hi_w2(NB_FF - 1)
                if ahead:
                    ahead()
                st, abase = (1, ACC_FF1) if f == 0 else (3, ACC_FF2)
                for c in range(KC):
                    act.wait_ge(acc_used.sem, acc_used.at(l, abase + 8 * (NB_FF - 1) + c + 1))
                    squares(l, st, c)
                roots(l, st)

            act.sem_inc(mcol_done.sem, 1)
            act.wait_ge(tables_in, 16)
            for n in range(0, 10, 2):
                act.wait_ge(xt_done, n + 1)
                t, q = n // 2, n % 2
                act.copy(xT[:, 4 * q:4 * q + 4, t * P:(t + 1) * P], bank(n % 4).rearrange("p (c t) -> p c t", c=4)).then_inc(xt_used, 1)
                act.wait_ge(xt_used, n + 2)
            act.wait_ge(cond_done, 1)
            act.activation(condE, bank(4, 16), ACT.Silu)
            act.activation(fcol, bank(4, 8, 16), ACT.Copy).then_inc(cond_exp, 1)

            act.wait_ge(x_ready, 1)
            for c in range(KC):
                squares(0, 0, c)
            roots(0, 0)

            def hi_first(l, f):
                for s in range(2):
                    for c in range(2):
                        hi_part(l, s, c, (RAW_FF1, RAW_FF2)[f], (0, un_ff2(2 * s + c))[f], "cols", f * OUT_BLOCKS[s])
            with act.Fori(0, DEPTH) as l:
                hi_first(l, 0)
                with act.Fori(0, MOD_AHEAD) as i:
                    modulation(l, i)
                def hi_cols(s, use, un_use, cs=(0, 1), kind="cols", extra=0):
                    for c in cs:
                        hi_part(l, s, c, RAW_MIX + use, UN_MIX + un_use, kind, extra)

                def evac(q, c, s, use):
                    u = 2 * s + c
                    act.wait_ge(unit_done[u].sem, unit_done[u].at(l, UN_MIX + use + 1))
                    act.copy(PT[:, bass.ds(q, 1), :].rearrange("p o t -> p (o t)"), pair(2 + c)).then_inc(acc_used.sem, 1)
                feed_forward(l, 0, lambda: hi_cols(0, 0, 0, kind="heads"))

                norm(l, 1)
                with act.Fori(0, 3) as i:
                    for s in range(3):
                        hi_cols((s + 1) % 3, i + (s + 1) // 3, i + (s + 1) // 3)
                        for c in range(2):
                            evac(6 * i + (2 * s + c), c, s, i)
                hi_cols(1, 3, 3, (0,))
                for c in range(2):
                    evac(18 + c, c, 0, 3)
                act.wait_ge(unit_done[2].sem, unit_done[2].at(l, UN_MIX + 4))
                act.copy(PS[0:64, :], pair(2)[0:64, :]).then_inc(acc_used.sem, 1)
                act.drain().then_inc(acc_used.sem, 1)
                act.drain().then_inc(proj_done.sem, 1)

                def fourier_features(c):
                    act.wait_ge(f1_done.sem, f1_done.at(l, c + 1))
                    if c:
                        act.wait_ge(f2_done.sem, f2_done.at(l, c))
                    act.copy(xcs, ps_all[:, 2816:4096].rearrange("p (t n) -> p t n", t=5)).then_inc(f1_used.sem, 1)

                def fourier_tokens(c):
                    act.wait_ge(f2_done.sem, f2_done.at(l, c + 1))
                    act.copy(hh[:, 6 + c, :].rearrange("p (t n) -> p t n", t=5), tiles5(4)).then_inc(f_hi.sem, 1)
                for n in range(3):
                    act.activation(sq7[:, n, :], PT[:, NORMS[n], :], ACT.Square)
                for n in range(6):
                    act.wait_ge(cv_ready.sem, cv_ready.at(l, n + 1))
                    act.activation(PT[:, C_QC + n, :], cv[:, n % 2, :], ACT.Silu).then_inc(cv_used.sem, 1)
                    if n < 4:
                        act.drain()
                        sq = act.activation(sq7[:, NORMS.index(C_QC + n), :], PT[:, C_QC + n, :], ACT.Square)
                    if n == 0:
                        fourier_features(0)
                    if n == 3:
                        sq.then_inc(sq7_ready.sem, 1)
                        fourier_tokens(0)
                act.activation(PT[:, C_ZC:C_ZC + 2, :], PT[:, C_ZC:C_ZC + 2, :], ACT.Silu)
                act.drain()
                act.wait_ge(nr_done.sem, nr_done.at(l, 1))
                act.activation(rrow[0:14, 1, :], pair(0)[0:14, :], ACT.Sqrt, bias=tb[0:14, T_SC + 1:T_SC + 2],
                               scale=tb[0:14, T_SC:T_SC + 1]).then_inc(nq_ready.sem, 1)
                fourier_features(1)
                act.wait_ge(ob_ready.sem, ob_ready.at(l, 1))
                act.copy(hh[:, 2:4, :], PT[:, C_GB:C_GB + 2, :]).then_inc(ob_hi.sem, 1)
                fourier_tokens(1)

                act.wait_ge(tr_done.sem, tr_done.at(l, 1))
                act.copy(vtok[:, 1:5, :], bank(0).rearrange("p (t n) -> p t n", t=4))
                act.copy(vtok[:, 5, :], bank(1, 128))
                act.copy(kct, bank(1, 128, 128))
                act.copy(kall[:, 0:P], bank(1, 128, 256)).then_inc(tr_used.sem, 1)

                def attend(n, latent, part="whole"):
                    w = T if latent else P

                    def exps(k, n=n):
                        act.wait_ge(nmax_ready.sem, nmax_ready.at(l, 4 * n + k + 1))
                        j = 4 * (k % 2)
                        act.activation(pexp[:, k % 2, 0:w], pair(k % 2)[:, 0:w], ACT.Exp, bias=ast[:, j + 1:j + 2],
                                       scale=HEAD ** -0.5, accum_out=ast[:, j + 2:j + 3]).then_inc(p_exp.sem, 1)

                    def out(k):
                        act.wait_ge(pT_done.sem, pT_done.at(l, 4 * n + k + 1))
                        if latent:
                            act.copy(pTs, tiles5(4)).then_inc(pT_used.sem, 1)
                        else:
                            act.copy(pTs[:, 0, :], tiles5(4)[:, 0, :]).then_inc(pT_used.sem, 1)
                    if part in ("whole", "first"):
                        exps(0)
                        exps(1)
                    if part == "first":
                        return
                    for k in range(4):
                        if k or latent:
                            act.wait_ge(pv_done.sem, pv_done.at(l, 4 * n + k))
                        out(k)
                        if k + 2 < 4:
                            exps(k + 2)
                        elif part == "middle":
                            exps(k - 2, n + 1)
                attend(0, False)
                attend(1, True, "first")
                with act.Fori(1, NT - 1) as i:
                    attend(i, True, "middle")
                attend(NT - 1, True, "last")

                act.activation(er, PS[0:8, :], ACT.Exp, scale=-1.0)
                act.activation(adt[32:40, 2:3], adt[32:40, 0:1], ACT.Exp).then_inc(e_rows.sem, 1)
                act.wait_ge(sp_x.sem, sp_x.at(l, 1))
                act.activation(PT[32:40, 9, :], PS[32:40, :], ACT.Abs)
                act.drain()
                act.activation(PT[32:40, 9, :], PT[32:40, 9, :], ACT.Exp, scale=-1.0)
                act.drain()
                act.activation(PT[32:40, 9, :], PT[32:40, 9, :], ACT.Ln, bias=ones[32:40, 0:1]).then_inc(e_ln.sem, 1)
                for k in range(4):
                    act.wait_ge(kv_done.sem, kv_done.at(l, k + 1))
                    act.copy((ktok, vtokc)[k // 2][:, k % 2], tiles5((4, 6)[k % 2])).then_inc(kv_used.sem, 1)
                act.wait_ge(gc_ready.sem, gc_ready.at(l, 1))
                act.activation(gk(G_EG), gk(G_GC), ACT.Exp)
                act.activation(gk(G_KD), gk(G_T), ACT.Exp)
                act.activation(gk(G_EGL), bank(1, 40, 40).rearrange("p (t e) -> p t e", t=NT), ACT.Exp).then_inc(gexp_ready.sem, 1)
                act.wait_ge(gr_done.sem, gr_done.at(l, 1))
                act.copy(gcr.rearrange("p (t n) -> p t n", t=5), tiles5(2)[0:8])
                act.activation(er.rearrange("p (t n) -> p t n", t=5), tiles5(2)[0:8], ACT.Exp).then_inc(gr_used.sem, 1)

                def delta(n):
                    for d in range(2):
                        b, e = dd[d], dv[d]
                        act.wait_ge(e["diff"].sem, e["diff"].at(l, n + 1))
                        act.activation(b["E"], b["E"], ACT.Exp).then_inc(e["decay"].sem, 1)
                    for lv in range(1, LEVELS):
                        for d in range(2):
                            b, e = dd[d], dv[d]
                            act.wait_ge(e["y"].sem, e["y"].at(l, (LEVELS - 1) * n + lv))
                            act.copy(b["Y"], bank(4 * d + 1).rearrange("p (h t) -> p h t", h=4)).then_inc(e["ye"].sem, 1)
                            if lv > 1:
                                act.wait_ge(e["p2"].sem, e["p2"].at(l, (LEVELS - 1) * n + lv - 1))
                                act.copy(b["TT"], bank(4 * d + 3).rearrange("p (h t) -> p h t", h=4)).then_inc(e["ye"].sem, 1)
                    for d in range(2):
                        b, e = dd[d], dv[d]
                        act.wait_ge(e["wt"].sem, e["wt"].at(l, n + 1))
                        act.mul(b["nwT"], bank(4 * d, 256).rearrange("p (c t) -> p c t", c=2), -1.0).then_inc(e["wte"].sem, 1)
                    for d in range(2):
                        b, e = dd[d], dv[d]
                        act.wait_ge(e["vn"].sem, e["vn"].at(l, n + 1))
                        act.copy(b["vnew"], bank(4 * d + 1, 256).rearrange("p (c t) -> p c t", c=2)).then_inc(e["vne"].sem, 1)
                delta(0)
                with act.Fori(1, NT) as i:
                    delta(i)
                act.wait_ge(oc_ready.sem, oc_ready.at(l, 1))
                act.activation(PT[:, 4:6, :], oC, ACT.Square).then_inc(sq7_ready.sem, 1)
                hi_cols(2, 3, 3, extra=1)
                act.wait_ge(nr_done.sem, nr_done.at(l, 2))
                act.activation(PT[0:14, 9, :], pair(0)[0:14, :], ACT.Sqrt, bias=tb[0:14, T_SC + 1:T_SC + 2],
                               scale=1.0 / HEAD).then_inc(nq_ready.sem, 1)
                act.wait_ge(oc_gate.sem, oc_gate.at(l, 1))
                act.copy(hh[:, 4:6, :], oC).then_inc(oc_hi.sem, 1)

                for j in range(1, 4):
                    s, use = (2, 0, 1, 2)[j], (3, 4, 4, 4)[j]
                    for c in range(2):
                        hi_cols(s, use, use - 1 if 2 * s + c == 3 else use, (c,), extra=j // 3 + 1)
                act.wait_ge(st_out.sem, st_out.at(l, 64))
                for c in range(KC):
                    if c == 6:
                        hi_first(l, 1)
                    act.wait_ge(acc_used.sem, acc_used.at(l, ACC_OUT + c + 1))
                    squares(l, 2, c)
                roots(l, 2)
                for n in range(MOD_STEPS - MOD_LATE, MOD_STEPS):
                    modulation(l, n)
                feed_forward(l, 1)

        @block.vector
        def _(ve):
            def lo_part(l, s, c, un_use, kind, frees):
                u = 2 * s + c
                ve.wait_ge(hi_done[u].sem, hi_done[u].at(l, un_use + 1))
                ve.tensor_tensor(un_view(un[u][1], kind), raw_view(s, c, kind), un_view(un[u][0], kind).bitcast(F32),
                                 ALU.subtract).then_inc(split_full[u].sem, 1)
                if frees:
                    ve.drain().then_inc(raw_free[s].sem, 1)

            def inverse_roots(l, st):
                for n, (lo, hi) in enumerate(HALVES):
                    ve.wait_ge(rt_ready.sem, rt_ready.at(l, 2 * st + n + 1))
                    ve.reciprocal(ssum[:, lo:hi], rt[:, lo:hi])
                ve.drain()

            def modulation(l, n):
                ve.wait_ge(mcol_done.sem, mcol_done.at(l, n + 1))
                settle(ve)
                ve.tensor_tensor(modT[:, bass.ds(4 * n, 4), :], mod_cols.rearrange("p (c s) -> p c s", c=4),
                                 vcol[:, bass.ds(4 * n, 4)].rearrange("p (c o) -> p c o", o=1).to_broadcast([P, 4, 2]),
                                 ALU.add).then_inc(mcol_used.sem, 1)

            def modulation_ready(st):
                gain = vcol[:, V_NORM + 8 * st:V_NORM + 8 * st + 8].rearrange("p (c o) -> p c o", o=1).to_broadcast([P, KC, 2])
                ve.scalar_tensor_tensor(mA[:, st], modT[:, 24 * st + 8:24 * st + 16, :], 1.0, gain, ALU.add, ALU.mult)
                if st != 1:
                    g = modT[:, 24 * st + 16:24 * st + 24, :]
                    ve.tensor_scalar(g, g, 0.5, None, ALU.mult)

            def norm(l, st):
                def scaled(c):
                    for s, lo, hi in STREAMS:
                        i = ve.scalar_tensor_tensor(t1[:, c % 2, lo:hi], xT[:, c, lo:hi], mA[:, st, c, s:s + 1], ssum[:, lo:hi],
                                                    ALU.mult, ALU.mult)
                    i.then_inc(t1_ready.sem, 1)
                scaled(0)
                scaled(1)
                for c in range(KC):
                    ve.wait_ge(hh_ready.sem, hh_ready.at(l, 8 * st + c + 1))
                    for s, lo, hi in STREAMS:
                        i = ve.scalar_tensor_tensor(hl[:, c, lo:hi], t1[:, c % 2, lo:hi], modT[:, 24 * st + c, s:s + 1],
                                                    hh[:, c, lo:hi].bitcast(F32), ALU.add, ALU.subtract)
                    i.then_inc(h_ready.sem, 1)
                    if c + 2 < KC:
                        ve.drain()
                        scaled(c + 2)

            def residual(o, q, gate_chunk):
                for s, lo, hi in STREAMS:
                    i = ve.scalar_tensor_tensor(xT[:, o, lo:hi], pair(q)[:, lo:hi], modT[:, gate_chunk + o, s:s + 1],
                                                xT[:, o, lo:hi], ALU.mult, ALU.add)
                i.then_inc(acc_used.sem, 1)

            def feed_forward(l, f, ahead=None):
                ub_ = [0] * 6 if f == 0 else [un_ff2(u) for u in range(6)]
                st = 0 if f == 0 else 2

                def lo_w13(i, c):
                    for s in range(2):
                        lo_part(l, s, c, ub_[2 * s + c] + i, "cols", c == 1)

                def lo_w2(i):
                    for g in range(2):
                        lo_part(l, 2, g, ub_[4 + g] + i, "rows", g == 1)

                def gated(i, c, q=1):
                    n = 2 * NB_FF * f + 2 * i + c
                    ve.wait_ge(sil_ready.sem, sil_ready.at(l, n + 1))
                    ve.wait_ge(unit_done[2 + c].sem, unit_done[2 + c].at(l, ub_[2 + c] + i + 1))
                    ve.tensor_tensor(gf[:, c, :], pair(q), sil[:, c, :], ALU.mult).then_inc(gf_ready.sem, 1)

                def gated_lo(i, c):
                    n = 2 * NB_FF * f + 2 * i + c
                    ve.wait_ge(gh_ready.sem, gh_ready.at(l, n + 1))
                    g = bass.ds(2 * (i % 2) + c, 1)
                    ve.tensor_tensor(gl[:, g, :].rearrange("p o t -> p (o t)"), gf[:, c, :],
                                     gh[:, g, :].rearrange("p o t -> p (o t)").bitcast(F32), ALU.subtract).then_inc(g_ready.sem, 1)

                def down(i, between=None):
                    for o in range(KC):
                        if between:
                            between(o)
                        if o < KC - 1:
                            ve.wait_ge(y_done.sem, y_done.at(l, 7 * NB_FF * f + 7 * i + o + 1))
                        else:
                            ve.wait_ge(unit_done[5].sem, unit_done[5].at(l, ub_[5] + i + 1))
                        residual(o, 2 + o % 2, 24 * st + 16)

                def step(i, more):
                    lo_w13(i, 1)
                    lo_w2(i - 1)
                    gated(i, 0)
                    gated_lo(i, 0)
                    if more:
                        lo_w13(i + 1, 0)
                    gated(i, 1)

                    def between(o):
                        if o == 0 and f == 0:
                            modulation(l, i + (MOD_AHEAD - 1))
                        if o == 2:
                            gated_lo(i, 1)
                    down(i - 1, between)
                norm(l, st)
                for c in range(2):
                    gated(0, c, 1 + 2 * c)
                    gated_lo(0, c)
                    if c == 0:
                        lo_w13(1, 0)
                with ve.Fori(1, NB_FF - 1) as i:
                    step(i, True)
                step(NB_FF - 1, False)
                lo_w2(NB_FF - 1)
                if f == 0:
                    ve.drain()
                    modulation_ready(1)
                    ve.drain()
                if ahead:
                    ahead()
                down(NB_FF - 1)

            for s in range(2):
                ve.sem_inc(acc_used.sem, 1)
            ve.wait_ge(tables_in, 16)
            for n in range(1, 10, 2):
                ve.wait_ge(xt_done, n + 1)
                t, q = n // 2, n % 2
                ve.wait_ge(xt_used, n)
                ve.tensor_copy(xT[:, 4 * q:4 * q + 4, t * P:(t + 1) * P], bank(n % 4).rearrange("p (c t) -> p c t", c=4)).then_inc(xt_used, 1)
            ve.wait_ge(cond_exp, 1)
            ve.wait_ge(vec_zero, 2)
            ve.tensor_copy(condP[:, :, 0:2], condE.rearrange("p (s k) -> p k s", s=2)).then_inc(cond_ready, 1)
            ve.drain().then_inc(x_ready, 1)
            ve.sem_inc(mcol_used.sem, 1)

            def lo_first(l, f, slots=(0, 1)):
                for s in slots:
                    for c in range(2):
                        lo_part(l, s, c, (0, un_ff2(2 * s + c))[f], "cols", c == 1)
            inverse_roots(0, 0)

            with ve.Fori(0, DEPTH) as l:
                ve.wait_ge(vecT_done.sem, vecT_done.at(l, 1))
                ve.tensor_copy(vcol, bank(6, 128))
                ve.drain().then_inc(cond_ready, 1)
                lo_first(l, 0)
                with ve.Fori(0, MOD_AHEAD) as i:
                    modulation(l, i)
                ve.drain()
                modulation_ready(0)
                ve.drain()
                def lo_cols(s, un_use, cs=(0, 1), kind="cols"):
                    for c in cs:
                        lo_part(l, s, c, UN_MIX + un_use, kind, c == cs[-1])
                feed_forward(l, 0, lambda: lo_cols(0, 0, kind="heads"))

                inverse_roots(l, 1)
                norm(l, 1)
                with ve.Fori(0, 3) as i:
                    for s in range(3):
                        lo_cols((s + 1) % 3, i + (s + 1) // 3)
                lo_cols(1, 3, (0,))

                ve.wait_ge(proj_done.sem, proj_done.at(l, 1))

                def conv(dst, src, w):
                    ve.tensor_scalar(dst, src, vcol[:, w(1):w(1) + 1], None, ALU.mult)
                    ve.drain()
                    for _, lo, hi in STREAMS:
                        ve.scalar_tensor_tensor(dst[:, lo + 1:hi], src[:, lo:hi - 1], vcol[:, w(0):w(0) + 1], dst[:, lo + 1:hi], ALU.mult, ALU.add)
                    ve.drain()
                    for _, lo, hi in STREAMS:
                        i = ve.scalar_tensor_tensor(dst[:, lo:hi - 1], src[:, lo + 1:hi], vcol[:, w(2):w(2) + 1], dst[:, lo:hi - 1], ALU.mult, ALU.add)
                    return i
                def fourier_lo(c):
                    ve.wait_ge(f_hi.sem, f_hi.at(l, c + 1))
                    ve.tensor_tensor(hl[:, 6 + c, :].rearrange("p (t n) -> p t n", t=5), tiles5(4),
                                     hh[:, 6 + c, :].rearrange("p (t n) -> p t n", t=5).bitcast(F32), ALU.subtract).then_inc(f_lo.sem, 1)
                for n in range(6):
                    if n >= 2:
                        ve.wait_ge(cv_used.sem, cv_used.at(l, n - 1))
                    conv(cv[:, n % 2, :], PT[:, C_QC + n, :], lambda j, n=n: V_CONVC + 6 * j + n).then_inc(cv_ready.sem, 1)
                for c in range(2):
                    if c:
                        fourier_lo(0)
                    ve.tensor_tensor(PT[:, C_XB + c, :], PT[:, C_XB + c, :], PT[:, C_GC + c, :], ALU.mult)
                    ve.drain()
                    conv(PT[:, C_GC + c, :], PT[:, C_XB + c, :], lambda j, c=c: V_CONVB + 2 * j + c)
                    ve.drain()
                    i = ve.tensor_tensor(PT[:, C_GB + c, :], PT[:, C_GB + c, :], PT[:, C_GC + c, :], ALU.mult)
                i.then_inc(ob_ready.sem, 1)

                ve.wait_ge(nq_ready.sem, nq_ready.at(l, 1))
                ve.reciprocal(rrow[0:14, 0, :], rrow[0:14, 1, :]).then_inc(nrow_ready.sem, 1)
                for n, c in enumerate(NORMS):
                    ve.wait_ge(bc_done.sem, bc_done.at(l, n + 1))
                    if n < 3:
                        v = V_QN if n < 2 else V_KN
                        i = ve.scalar_tensor_tensor(PT[:, c, :], PT[:, c, :], vcol[:, v:v + 1], pair(n % 2), ALU.mult, ALU.mult)
                    else:
                        i = ve.tensor_tensor(PT[:, c, :], PT[:, c, :], pair(n % 2), ALU.mult)
                    i.then_inc(bc_used.sem, 1)
                ve.wait_ge(ob_hi.sem, ob_hi.at(l, 1))
                ve.tensor_tensor(hl[:, 2:4, :], PT[:, C_GB:C_GB + 2, :], hh[:, 2:4, :].bitcast(F32), ALU.subtract)
                fourier_lo(1)

                ve.wait_ge(mt_in.sem, mt_in.at(l, 80))
                for n, c in enumerate((C_QA, C_QA + 1, C_KA)):
                    ve.wait_ge(rot_done.sem, rot_done.at(l, n + 1))
                    ve.tensor_tensor(rtmp, bank((2, 3, 6)[n]), ub[:, U_SIN:U_SIN + 512], ALU.mult)
                    ve.tensor_tensor(PT[:, c, CTX:T], PT[:, c, CTX:T], ub[:, U_COS:U_COS + 512], ALU.mult)
                    ve.drain()
                    i = ve.tensor_tensor(kall[:, CTX:T] if c == C_KA else PT[:, c, CTX:T], PT[:, c, CTX:T], rtmp, ALU.add)
                    ve.drain()
                ve.drain().then_inc(roped.sem, 1)

                def attend(n, t, latent, part="whole"):
                    w = T if latent else P

                    def queries(t):
                        ve.tensor_copy(qs, PT[:, C_QA:C_QA + 2, bass.ds(t * P, P)]).then_inc(qs_ready.sem, 1)

                    def peak(k, n=n):
                        j = 4 * (k % 2)
                        ve.wait_ge(s_done.sem, s_done.at(l, 4 * n + k + 1))
                        ve.tensor_reduce(ast[:, j:j + 1], pair(k % 2)[:, 0:w], AX.X, ALU.max)
                        ve.drain()
                        ve.tensor_scalar(ast[:, j + 1:j + 2], ast[:, j:j + 1], -HEAD ** -0.5, None, ALU.mult).then_inc(nmax_ready.sem, 1)

                    def scale(k):
                        j = 4 * (k % 2)
                        ve.wait_ge(p_exp.sem, p_exp.at(l, 4 * n + k + 1))
                        ve.reciprocal(ast[:, j + 3:j + 4], ast[:, j + 2:j + 3])
                        ve.drain()
                        ve.tensor_scalar(pexp[:, k % 2, 0:w], pexp[:, k % 2, 0:w], ast[:, j + 3:j + 4], None, ALU.mult).then_inc(p_ready.sem, 1)

                    def heads_out(c):
                        ve.wait_ge(pv_done.sem, pv_done.at(l, 4 * n + 2 * c + 2))
                        o = bank(6 + c, 128)
                        hs = hh[:, c, bass.ds(t * P, P)]
                        ve.tensor_copy(hs, o)
                        ve.drain()
                        ve.tensor_tensor(hl[:, c, bass.ds(t * P, P)], o, hs.bitcast(F32), ALU.subtract).then_inc(pv_used.sem, 1)
                    if part in ("whole", "first"):
                        queries(t)
                        peak(0)
                        peak(1)
                    if part == "first":
                        return
                    for k in range(4):
                        scale(k)
                        if k + 2 < 4:
                            peak(k + 2)
                            if k == 1 and part == "middle":
                                queries(t + 1)
                        elif part == "middle":
                            peak(k - 2, n + 1)
                        if k == 2:
                            heads_out(0)
                    heads_out(1)
                attend(0, 0, False)
                attend(1, 1, True, "first")
                with ve.Fori(1, NT - 1) as i:
                    attend(i, i, True, "middle")
                attend(NT - 1, NT - 1, True, "last")

                ve.tensor_scalar(PS[32:40, :], PS[32:40, :], adt[32:40, 1:2], None, ALU.add).then_inc(sp_x.sem, 1)
                ve.wait_ge(e_rows.sem, e_rows.at(l, 1))
                ve.tensor_scalar(er, er, 1.0, None, ALU.add)
                ve.drain()
                ve.reciprocal(PS[0:8, :], er)
                ve.wait_ge(e_ln.sem, e_ln.at(l, 1))
                ve.scalar_tensor_tensor(PS[32:40, :], PS[32:40, :], 0.0, PT[32:40, 9, :], ALU.max, ALU.add)
                ve.drain()
                ve.tensor_scalar(PS[32:40, :], PS[32:40, :], adt[32:40, 2:3], -1.0, ALU.mult, ALU.mult).then_inc(rows_ready.sem, 1)
                ve.wait_ge(gt_done.sem, gt_done.at(l, 1))
                ve.tensor_copy(gsm[:, 0:40], bank(0, 40))
                ve.tensor_copy(gsm[:, 40:80], bank(2, 40)).then_inc(gt_used.sem, 1)
                ve.wait_ge(gc_done.sem, gc_done.at(l, 1))
                ve.tensor_copy(gk(G_GC), bank(1, 40).rearrange("p (t e) -> p t e", t=NT))
                ve.drain()
                ve.tensor_tensor(gk(G_T), bank(1, 40, 40).rearrange("p (t e) -> p t e", t=NT), gk(G_GC), ALU.subtract)
                ve.drain()
                ve.tensor_scalar(gk(G_T), gk(G_T), 0.0, None, ALU.min).then_inc(gc_ready.sem, 1)
                ve.wait_ge(gexp_ready.sem, gexp_ready.at(l, 1))
                ve.tensor_tensor(gk(G_BG), gk(G_BETA), gk(G_EG), ALU.mult)
                ve.drain().then_inc(gcol_ready.sem, 1)
                ve.wait_ge(kv_used.sem, kv_used.at(l, 4))
                ve.wait_ge(gr_used.sem, gr_used.at(l, 1))
                ve.wait_ge(oz_ready.sem, oz_ready.at(l, 1))

                def delta(tiles, n, St):
                    cols = [bass.ds(t * P, P) for t in tiles]
                    ds1 = [bass.ds(t, 1) for t in tiles]
                    b4 = lambda d, k: bank(4 * d + k).rearrange("p (h t) -> p h t", h=4)
                    id4 = ident.rearrange("p (o n) -> p o n", o=1).to_broadcast([P, 4, P])

                    def col(k, d, h, p0=0, p1=P):
                        c = gsm[p0:p1, 40 * k:40 * k + 40].rearrange("p (t e) -> p t e", t=NT)
                        return c[:, ds1[d], 4 * d + h:4 * d + h + 1].rearrange("p o e -> p (o e)")
                    for d in range(2):
                        b, e = dd[d], dv[d]
                        ve.wait_ge(e["bcast"].sem, e["bcast"].at(l, n + 1))
                        settle(ve)
                        for h in range(4):
                            i = ve.scalar_tensor_tensor(b["E"][:, h, :], b4(d, 0)[:, h, :], col(G_GC, d, h), negm(d), ALU.subtract, ALU.min)
                        i.then_inc(e["diff"].sem, 1)
                        bb = bank(4 * d + 1).rearrange("p (k c t) -> p k c t", k=2, c=2)
                        ve.tensor_copy(b["kst"], PT[:, C_KC:C_KC + 2, cols[d]])
                        ve.tensor_copy(b["qst"], PT[:, C_QC:C_QC + 2, cols[d]])
                        ve.tensor_tensor(b["qg"], bb[:, 0], PT[:, C_QC:C_QC + 2, cols[d]], ALU.mult)
                        ve.tensor_tensor(b["kbT"], bb[:, 1], PT[:, C_KC:C_KC + 2, cols[d]], ALU.mult).then_inc(e["staged"].sem, 1)
                    for d in range(2):
                        b, e = dd[d], dv[d]
                        ve.wait_ge(e["decay"].sem, e["decay"].at(l, n + 1))
                        ve.wait_ge(e["gram"].sem, e["gram"].at(l, n + 1))
                        gram = ps_all[:, (4 * d + 2) * 512:(4 * d + 4) * 512].rearrange("p (g k c t) -> p k c g t", g=2, k=2, c=2)
                        cg = lambda x: x.rearrange("p (c g) t -> p c g t", c=2)
                        ve.tensor_tensor(cg(b["LT"]), gram[:, 1], cg(b["E"]), ALU.mult).then_inc(e["lt"].sem, 1)
                    for d in range(2):
                        b, e = dd[d], dv[d]
                        gram = ps_all[:, (4 * d + 2) * 512:(4 * d + 4) * 512].rearrange("p (g k c t) -> p k c g t", g=2, k=2, c=2)
                        ve.tensor_tensor(cg(b["AQ"]), gram[:, 0], cg(b["E"]), ALU.mult)
                    for d in range(2):
                        b, e = dd[d], dv[d]
                        ve.wait_ge(e["b1"].sem, e["b1"].at(l, n + 1))
                        ve.tensor_tensor(b["T"], id4, b4(d, 0), ALU.subtract).then_inc(e["tt"].sem, 1)
                        ve.tensor_tensor(b["TT"], id4, b["B0"], ALU.subtract).then_inc(e["tt"].sem, 1)
                        for src, k, dst in ((ktok, G_BG, "kbg"), (vtokc, G_BETA, "vb"), (ktok, G_KD, "kdec")):
                            g = gk(k)[:, ds1[d], 4 * d:4 * d + 4].rearrange("p o h -> p (o h)").rearrange("p (c g u) -> p c g u", c=2, g=2)
                            i = ve.tensor_tensor(b[dst].rearrange("p c (g n) -> p c g n", g=2),
                                                 src[:, :, ds1[d], :].rearrange("p c o n -> p c (o n)").rearrange("p c (g n) -> p c g n", g=2),
                                                 g.to_broadcast([P, 2, 2, HEAD]), ALU.mult)
                        i.then_inc(e["kb"].sem, 1)
                    for lv in range(1, LEVELS):
                        for d in range(2):
                            b, e = dd[d], dv[d]
                            if lv < LEVELS - 1:
                                ve.wait_ge(e["p1"].sem, e["p1"].at(l, (LEVELS - 2) * n + lv))
                                ve.tensor_tensor(b["T"], b["T"], b4(d, 2), ALU.subtract).then_inc(e["tt"].sem, 1)
                            else:
                                ve.wait_ge(e["p2"].sem, e["p2"].at(l, (LEVELS - 1) * n + lv))
                                ve.tensor_tensor(b["TT"], b["TT"], b4(d, 3), ALU.subtract).then_inc(e["tt"].sem, 1)
                    for d in range(2):
                        b, e = dd[d], dv[d]
                        ve.wait_ge(e["os"].sem, e["os"].at(l, n + 1))
                        ve.tensor_tensor(oC[:, :, cols[d]], oC[:, :, cols[d]], bank(4 * d + 2, 256).rearrange("p (c t) -> p c t", c=2), ALU.add)
                        for c in range(2):
                            for g in range(2):
                                r = slice(64 * g, 64 * g + 64)
                                sv = St[r, d, c, r]
                                i = ve.scalar_tensor_tensor(sv, sv, col(G_EGL, d, 2 * c + g, 64 * g, 64 * g + 64),
                                                            ps_all[r, (4 * d + 3) * 512 + 128 * c + 64 * g:(4 * d + 3) * 512 + 128 * c + 64 * g + 64],
                                                            ALU.mult, ALU.add)
                        i.then_inc(e["ose"].sem, 1)
                        ve.drain()
                delta((0, 0), 0, Sctx)
                ve.wait_ge(st_in, 48 + 64 * (l + 1))
                settle(ve)
                with ve.Fori(1, NT) as i:
                    delta((i, NT - i), i, Slat)
                ve.drain().then_inc(oc_ready.sem, 1)
                lo_cols(2, 3)

                ve.wait_ge(nq_ready.sem, nq_ready.at(l, 2))
                ve.reciprocal(PT[0:14, 8, :], PT[0:14, 9, :]).then_inc(nrow_ready.sem, 1)
                for c in range(2):
                    ve.wait_ge(bc_done.sem, bc_done.at(l, 8 + c))
                    ve.scalar_tensor_tensor(oC[:, c, :], oC[:, c, :], vcol[:, V_DN:V_DN + 1], pair(c % 2), ALU.mult, ALU.mult).then_inc(bc_used.sem, 1)
                ve.drain()
                ve.tensor_tensor(oC, oC, PT[:, C_ZC:C_ZC + 2, :], ALU.mult).then_inc(oc_gate.sem, 1)
                ve.wait_ge(oc_hi.sem, oc_hi.at(l, 1))
                ve.tensor_tensor(hl[:, 4:6, :], oC, hh[:, 4:6, :].bitcast(F32), ALU.subtract).then_inc(oc_lo.sem, 1)

                for j in range(1, 4):
                    s, use = (2, 0, 1, 2)[j], (3, 4, 4, 4)[j]
                    for c in range(2):
                        lo_part(l, s, c, UN_MIX + (use - 1 if 2 * s + c == 3 else use), "cols", c == 1)
                    out_residual(ve, l, j - 1, residual, unit_done)
                lo_first(l, 1, (0,))
                out_residual(ve, l, 3, residual, unit_done)
                lo_first(l, 1, (1,))
                ve.wait_ge(st_out.sem, st_out.at(l, 64))
                inverse_roots(l, 2)
                for n in range(MOD_STEPS - MOD_LATE, MOD_STEPS):
                    modulation(l, n)
                ve.drain()
                modulation_ready(2)
                ve.drain()
                feed_forward(l, 1)
                inverse_roots(l, 3)

            for c in range(KC):
                ve.scalar_tensor_tensor(xT[:, c, :], xT[:, c, :], fcol[:, c:c + 1], ssum, ALU.mult, ALU.mult).then_inc(fin_x, 1)
            n = 0
            for t in range(NT):
                for q in range(2):
                    ve.wait_ge(fin_t, n + 1)
                    ve.tensor_copy(fin_row[:, t, 512 * q:512 * q + 512], bank(n % 4)).then_inc(fin_e, 1)
                    n += 1


def out_residual(ve, l, j, residual, unit_done):
    s, use = (2, 0, 1, 2)[j], (3, 4, 4, 4)[j]
    for c in range(2):
        u = 2 * s + c
        ve.wait_ge(unit_done[u].sem, unit_done[u].at(l, UN_MIX + (use - 1 if u == 3 else use) + 1))
        residual(2 * j + c, 2 + c, 24 + 16)


def _tables():
    import numpy as np
    p = np.arange(P)
    tb = np.zeros((P, T_ALL))
    tb[:, T_ID:T_ID + P] = np.eye(P)
    tb[:, T_ONE:T_ONE + P] = 1
    j, i = p[:, None], p[None, :]
    for lv in range(LEVELS):
        n = 2 ** lv
        m = ((i // (2 * n)) == (j // (2 * n))) & (j // n % 2 == 0) & (i // n % 2 == 1)
        tb[:, T_MASK + lv * P:T_MASK + (lv + 1) * P] = m
        tb[:, T_MASK + (LEVELS + lv) * P:T_MASK + (LEVELS + lv + 1) * P] = m.T
    tb[:, T_NEG:T_NEG + P] = np.where(i >= j, 0, -1e30)
    tb[:, T_NEG + P:T_NEG + 2 * P] = np.where(i <= j, 0, -1e30)
    tb[:, T_TRI:T_TRI + P] = j <= i
    tb[:, T_TRI + P:T_TRI + 2 * P] = j >= i
    for c in range(7):
        for g in range(2):
            r = 2 * c + g
            tb[64 * g:64 * g + 64, T_SUM + 14 * c + r] = 1
            tb[r, T_BC + 128 * c + 64 * g:T_BC + 128 * c + 64 * g + 64] = HEAD ** -0.5 if c >= 5 else 1
            tb[r, T_SC] = 1.0 / HEAD if c < 3 else 1
    tb[:, T_SC + 1] = EPS
    for g in range(4):
        for s in range(2):
            tb[32 * g + s, T_SEL + s] = 1
    q = HEAD // 4
    rot = np.zeros((P, P))
    for m in range(P):
        if m % (2 * q) < q:
            rot[m + q, m] = -1
        else:
            rot[m - q, m] = 1
    tb[:, T_ROT:T_ROT + P] = rot
    ub = np.zeros((P, U_ALL))
    inv = (np.float32(10000.0) ** (-np.arange(q, dtype=np.float32) / np.float32(q))).astype(np.float32)
    tok = np.arange(LAT)
    for m in range(P):
        f = m % HEAD
        pos = (tok // 64 if f < HEAD // 2 else tok % 64).astype(np.float32)
        ang = (pos * inv[f % q]).astype(np.float32).astype(np.float64)
        ub[m, U_COS:U_COS + LAT] = np.cos(ang)
        ub[m, U_SIN:U_SIN + LAT] = np.sin(ang)
    f = np.arange(HEAD)
    w = 2 * np.pi * (f[:, None] * f[None, :] % HEAD) / HEAD
    for g in range(2):
        r = slice(64 * g, 64 * g + 64)
        ub[r, U_DFT + 64 * g:U_DFT + 64 * g + 64] = np.cos(w)
        ub[r, U_DFT + P + 64 * g:U_DFT + P + 64 * g + 64] = np.sin(w)
    for n, uc, us in ((LAT, U_CL, U_SL), (CTX, U_CC, U_SCX)):
        k = np.arange(n)
        w = 2 * np.pi * (k[:, None] * k[None, :] % n) / n
        s = 1 / np.sqrt(n * HEAD)
        for t in range(n // P):
            ub[:, uc + t * n:uc + (t + 1) * n] = np.cos(w[t * P:(t + 1) * P]) * s
            ub[:, us + t * n:us + (t + 1) * n] = -np.sin(w[t * P:(t + 1) * P]) * s
    return tb.astype(np.float32), ub.astype(np.float32)


_INS = ["x_prompt", "x_sample", "c", "cache_k", "cache_v", "state_delta", "c_ctx", "mod_w", "mod_b", "norm_ffn1", "norm_mix",
        "norm_ffn2", "ffn1_w1", "ffn1_w3", "ffn1_w2", "ffn2_w1", "ffn2_w3", "ffn2_w2", "w_in", "w_out", "q_norm", "k_norm",
        "conv_b_w", "conv_c_w", "delta_a_log", "delta_dt_bias", "delta_norm", "final_norm"]
_OUTS = [(1, CTX, D), (1, LAT, D), (1, DEPTH, 2, CTX, HEAD), (1, DEPTH, 2, CTX, HEAD), (1, DEPTH, 2, 4, HEAD, HEAD)]


def kernel(**inputs):
    import numpy as np
    import concourse.bacc as bacc
    from concourse.bass_utils import run_bass_kernel_spmd

    nc = bacc.Bacc("TRN2", target_bir_lowering=False, num_devices=1)
    arrays, args = {}, {}
    for name in _INS:
        arrays[name] = np.ascontiguousarray(inputs[name])
        args[name] = nc.dram_tensor(name, arrays[name].shape, F32, kind="ExternalInput").ap()
    extra = []
    for name, value in zip(("tables", "mixer_tables"), _tables()):
        arrays[name] = value
        extra.append(nc.dram_tensor(name, value.shape, F32, kind="ExternalInput").ap())
    outs = [nc.dram_tensor(f"out{i}", shape, F32, kind="ExternalOutput").ap() for i, shape in enumerate(_OUTS)]
    build(nc, args, *extra, outs)
    r = run_bass_kernel_spmd(nc, [arrays], core_ids=[0])
    return tuple(r.results[0][f"out{i}"] for i in range(len(_OUTS)))
```
